# Optimizing a Trainium2 kernel written in Bass

```python
import jax, jax.numpy as jnp
from jax import lax
import numpy as np

D_MODEL = 1024
BATCH = 1
SEQ = 1024
DEPTH = 1

ATTN_GROUPS = ((128, 1), (512, 4), (2048, 16))
N_ATTN_GROUPS = len(ATTN_GROUPS)
ATTN_HEADS_PER_GROUP = 4
ATTN_HEADS = N_ATTN_GROUPS * ATTN_HEADS_PER_GROUP
ATTN_HEAD_DIM = 128
ATTN_OUT_WIDTH = ATTN_HEADS_PER_GROUP * ATTN_HEAD_DIM
ROPE_THETA = 500000.0
ROPE_DIM = ATTN_HEAD_DIM // 4
GLA_HEADS = 4
GLA_KEY_DIM = (D_MODEL // 2) // GLA_HEADS
GLA_VAL_DIM = D_MODEL // GLA_HEADS
GLA_GATE_RANK = 16
GLA_GATE_NORMALIZER = 16.0
GLA_CHUNK = 64
FFN_HIDDEN = -(-8 * D_MODEL // (3 * 256)) * 256
NORM_EPS = 1e-6

IN_SIZES = (ATTN_HEADS * ATTN_HEAD_DIM,
            ATTN_HEADS * ATTN_HEAD_DIM,
            ATTN_HEADS * ATTN_HEAD_DIM,
            GLA_HEADS * GLA_KEY_DIM,
            GLA_HEADS * GLA_KEY_DIM,
            GLA_HEADS * GLA_VAL_DIM,
            GLA_HEADS * GLA_VAL_DIM,
            GLA_GATE_RANK,
            D_MODEL,
            D_MODEL)
IN_WIDTH = int(sum(IN_SIZES))
IN_SPLIT_POINTS = tuple(int(v) for v in np.cumsum(IN_SIZES)[:-1])

kernel_name = "hybrid_dilated_swa_gla_block"

def rmsnorm(x, g):
    xf = x.astype(jnp.float32)
    y = xf * lax.rsqrt(jnp.mean(xf * xf, axis=-1, keepdims=True) + NORM_EPS)
    return (y * g.astype(jnp.float32)).astype(x.dtype)

def rope_tables(seq_len):
    inv_freq = ROPE_THETA ** (-jnp.arange(0, ROPE_DIM, 2, dtype=jnp.float32) / ROPE_DIM)
    ang = jnp.arange(seq_len, dtype=jnp.float32)[:, None] * inv_freq[None, :]
    ang = jnp.concatenate([ang, ang], axis=-1)[None, :, None, :]
    return jnp.cos(ang), jnp.sin(ang)

def partial_rope(t, cos, sin):
    rot = t[..., :ROPE_DIM].astype(jnp.float32)
    half = ROPE_DIM // 2
    rotated = jnp.concatenate([-rot[..., half:], rot[..., :half]], axis=-1)
    rot = rot * cos + rotated * sin
    return jnp.concatenate([rot.astype(t.dtype), t[..., ROPE_DIM:]], axis=-1)

def dilated_window_attention(q, k, v, dilation, keys_back):
    B, S, H, Dh = q.shape
    r, blk = dilation, keys_back
    L = S // r
    nb = -(-L // blk)
    Lp = nb * blk

    def to_sub(t):
        t = t.reshape(B, L, r, H, Dh).transpose(0, 2, 3, 1, 4)
        t = jnp.pad(t, ((0, 0), (0, 0), (0, 0), (0, Lp - L), (0, 0)))
        return t.reshape(B, r, H, nb, blk, Dh)

    def with_prev(t):
        prev = jnp.pad(t, ((0, 0), (0, 0), (0, 0), (1, 0), (0, 0), (0, 0)))[:, :, :, :-1]
        return jnp.concatenate([prev, t], axis=4)

    qb = to_sub(q)
    kk = with_prev(to_sub(k))
    vv = with_prev(to_sub(v))
    scores = jnp.einsum('brhnqd,brhnkd->brhnqk', qb, kk).astype(jnp.float32) * (Dh ** -0.5)
    qi = jnp.arange(blk)[:, None]
    kj = jnp.arange(2 * blk)[None, :] - blk
    dist = qi - kj
    blk_idx = jnp.arange(nb)[:, None, None]
    valid = (dist >= 0)[None] & (dist <= keys_back)[None] & ((blk_idx > 0) | (kj >= 0)[None])
    scores = jnp.where(valid, scores, -jnp.inf)
    m = jnp.max(scores, axis=-1)
    p = jnp.exp(scores - m[..., None])
    l = jnp.sum(p, axis=-1)
    o = jnp.einsum('brhnqk,brhnkd->brhnqd', p, vv.astype(jnp.float32)) / l[..., None]

    def from_sub(t):
        rest = t.shape[5:]
        t = t.reshape((B, r, H, Lp) + rest)[:, :, :, :L]
        t = t.transpose((0, 3, 1, 2) + tuple(range(4, 4 + len(rest))))
        return t.reshape((B, S, H) + rest)

    return from_sub(o), from_sub(m), from_sub(l)

def dilated_attention_mixer(q, k, v):
    B, S = q.shape[:2]
    outs, maxes, dens = [], [], []
    for g, (window, dilation) in enumerate(ATTN_GROUPS):
        sl = slice(g * ATTN_HEADS_PER_GROUP, (g + 1) * ATTN_HEADS_PER_GROUP)
        o, m, l = dilated_window_attention(q[:, :, sl], k[:, :, sl], v[:, :, sl],
                                           dilation, window // dilation)
        outs.append(o); maxes.append(m); dens.append(l)
    o = jnp.stack(outs, 0)
    m = jnp.stack(maxes, 0)
    l = jnp.stack(dens, 0)
    w = l * jnp.exp(m - jnp.max(m, axis=0, keepdims=True))
    out = jnp.sum(w[..., None] * o, axis=0) / jnp.sum(w, axis=0)[..., None]
    return out.reshape(B, S, ATTN_OUT_WIDTH)

def gla_chunked(q, k, v, log_a):
    B, S, H, dk = q.shape
    dv = v.shape[-1]
    C = GLA_CHUNK
    N = S // C
    q = q.reshape(B, N, C, H, dk) * (dk ** -0.5)
    k = k.reshape(B, N, C, H, dk)
    v = v.reshape(B, N, C, H, dv)
    b = jnp.cumsum(log_a.reshape(B, N, C, H, dk), axis=2)
    b_last = b[:, :, -1]
    b_ref = b[:, :, C // 2:C // 2 + 1]
    A = jnp.einsum('bnihd,bnjhd->bnhij', q * jnp.exp(b - b_ref), k * jnp.exp(b_ref - b))
    causal = jnp.tril(jnp.ones((C, C), dtype=bool))
    o_intra = jnp.einsum('bnhij,bnjhv->bnihv', jnp.where(causal, A, 0.0), v)
    q_inter = q * jnp.exp(b)
    k_state = k * jnp.exp(b_last[:, :, None] - b)
    decay = jnp.exp(b_last)

    def step(state, inp):
        qc, kc, vc, dc = inp
        o = jnp.einsum('bihd,bhdv->bihv', qc, state)
        state = dc[..., None] * state + jnp.einsum('bjhd,bjhv->bhdv', kc, vc)
        return state, o

    xs = (jnp.moveaxis(q_inter, 1, 0), jnp.moveaxis(k_state, 1, 0),
          jnp.moveaxis(v, 1, 0), jnp.moveaxis(decay, 1, 0))
    state0 = jnp.zeros((B, H, dk, dv), jnp.float32)
    _, o_inter = lax.scan(step, state0, xs)
    o = o_intra + jnp.moveaxis(o_inter, 0, 1)
    return o.reshape(B, S, H, dv)

def setup_inputs(seed: int = 0) -> dict:
    key = jax.random.key(seed)
    ks = jax.random.split(key, 16)
    f32 = jnp.float32
    nrm = lambda k, shape, fan_in: jax.random.normal(k, shape, f32) * (fan_in ** -0.5)
    gain = lambda k, shape: 1.0 + 0.01 * jax.random.normal(k, shape, f32)
    return {
        "x": jax.random.normal(ks[0], (BATCH, SEQ, D_MODEL), f32),
        "norm1_g": gain(ks[1], (DEPTH, D_MODEL)),
        "w_in": nrm(ks[2], (DEPTH, D_MODEL, IN_WIDTH), D_MODEL),
        "w_gate_lr": nrm(ks[3], (DEPTH, GLA_GATE_RANK, GLA_HEADS * GLA_KEY_DIM), GLA_GATE_RANK),
        "b_gate": 0.01 * jax.random.normal(ks[4], (DEPTH, GLA_HEADS * GLA_KEY_DIM), f32),
        "gla_norm_g": gain(ks[5], (DEPTH, GLA_VAL_DIM)),
        "w_branch_a": nrm(ks[6], (DEPTH, ATTN_OUT_WIDTH, D_MODEL), ATTN_OUT_WIDTH),
        "w_branch_b": nrm(ks[7], (DEPTH, GLA_HEADS * GLA_VAL_DIM, D_MODEL), GLA_HEADS * GLA_VAL_DIM),
        "w_out": nrm(ks[8], (DEPTH, D_MODEL, D_MODEL), D_MODEL),
        "norm2_g": gain(ks[9], (DEPTH, D_MODEL)),
        "w_ffn_in": nrm(ks[10], (DEPTH, D_MODEL, 2 * FFN_HIDDEN), D_MODEL),
        "w_ffn_down": nrm(ks[11], (DEPTH, FFN_HIDDEN, D_MODEL), FFN_HIDDEN),
        "norm_f_g": gain(ks[12], (D_MODEL,)),
    }

def reference(x, norm1_g, w_in, w_gate_lr, b_gate, gla_norm_g, w_branch_a, w_branch_b,
              w_out, norm2_g, w_ffn_in, w_ffn_down, norm_f_g):
    B, S, D = x.shape
    cos, sin = rope_tables(S)
    for layer in range(DEPTH):
        h = rmsnorm(x, norm1_g[layer])
        proj = h @ w_in[layer]
        aq, ak, av, gq, gk, gv, gr, glr, ga, gb = jnp.split(proj, IN_SPLIT_POINTS, axis=-1)

        aq = partial_rope(aq.reshape(B, S, ATTN_HEADS, ATTN_HEAD_DIM), cos, sin)
        ak = partial_rope(ak.reshape(B, S, ATTN_HEADS, ATTN_HEAD_DIM), cos, sin)
        av = av.reshape(B, S, ATTN_HEADS, ATTN_HEAD_DIM)
        attn_out = dilated_attention_mixer(aq, ak, av).astype(x.dtype)

        log_a = jax.nn.log_sigmoid((glr @ w_gate_lr[layer] + b_gate[layer]).astype(jnp.float32))
        log_a = (log_a / GLA_GATE_NORMALIZER).reshape(B, S, GLA_HEADS, GLA_KEY_DIM)
        o_gla = gla_chunked(gq.reshape(B, S, GLA_HEADS, GLA_KEY_DIM).astype(jnp.float32),
                            gk.reshape(B, S, GLA_HEADS, GLA_KEY_DIM).astype(jnp.float32),
                            gv.reshape(B, S, GLA_HEADS, GLA_VAL_DIM).astype(jnp.float32),
                            log_a)
        o_gla = rmsnorm(o_gla, gla_norm_g[layer])
        o_gla = o_gla * jax.nn.silu(gr.reshape(B, S, GLA_HEADS, GLA_VAL_DIM).astype(jnp.float32))
        gla_out = o_gla.reshape(B, S, GLA_HEADS * GLA_VAL_DIM).astype(x.dtype)

        mix = (jax.nn.sigmoid(ga) * (attn_out @ w_branch_a[layer])
               + jax.nn.sigmoid(gb) * (gla_out @ w_branch_b[layer]))
        x = x + mix @ w_out[layer]

        h2 = rmsnorm(x, norm2_g[layer])
        g, u = jnp.split(h2 @ w_ffn_in[layer], 2, axis=-1)
        x = x + (jax.nn.silu(g) * u) @ w_ffn_down[layer]
    return rmsnorm(x, norm_f_g)


_drawn_inputs = setup_inputs


def setup_inputs(seed=0):
    import zlib

    import numpy as np

    out = dict(_drawn_inputs(seed))
    spreads = {}
    factors = {'norm1_g': 6.864,
     'b_gate': 28.59,
     'gla_norm_g': 33.118,
     'norm2_g': 37.019,
     'norm_f_g': 33.346}
    for name, (base, spread) in spreads.items():
        noise = np.random.default_rng([zlib.crc32(name.encode()), seed]).standard_normal(out[name].shape)
        drawn = base * np.exp(spread * noise) if base else spread * noise
        out[name] = __import__('jax').numpy.asarray(drawn.astype(out[name].dtype))
    for name, factor in factors.items():
        out[name] = (out[name] * factor).astype(out[name].dtype)
    return out
```

```python
from contextlib import ExitStack

import numpy as np
import concourse.bass as bass
from concourse import mybir

ALU = mybir.AluOpType
ACT = mybir.ActivationFunctionType
AX = mybir.AxisListType
F32 = mybir.dt.float32
F32R = mybir.dt.float32r
I32 = mybir.dt.int32

P = 128
S = 1024
D = 1024
KC = D // P
TT = S // P
HALF = 512
HD = 128
HEADS = 4
GROUPS = 3
DIL = (1, 4, 16)
ROPE = HD // 4
ROPE_THETA = 500000.0
GV = 256
CH = 64
RANK = 16
GATE_NORM = 16.0
FFN = 2816
EPS = 1e-6
BIG = 1e30

AQ, AK, AV = 0, 1536, 3072
GQ, GK, GVC, GR, GLR, GA, GB = 4608, 5120, 5632, 6656, 7680, 7696, 8720

C_ID, C_BAND, C_PAIR, C_GLA, C_RESTART, C_END = 0, 128, 384, 512, 640, 1152


def shape_constants():
    q, k = np.arange(P)[:, None], np.arange(P)[None, :]
    blob = np.zeros((P, C_END), np.float32)
    blob[:, C_ID:C_ID + P] = q == k
    blob[:, C_BAND:C_BAND + P] = np.where(k >= q, 0.0, -BIG)
    blob[:, C_BAND + P:C_BAND + 2 * P] = np.where(k <= q, 0.0, -BIG)
    blob[:, C_PAIR:C_PAIR + P] = np.where((k <= q) & (k % 2 == q % 2), 0.0, -BIG)
    blob[:, C_GLA:C_GLA + P] = q <= k
    blob[:, C_RESTART:C_END] = (np.arange(C_END - C_RESTART) % CH != 0)[None, :]
    inv = np.float32(ROPE_THETA) ** (-np.arange(0, ROPE, 2, dtype=np.float32) / np.float32(ROPE))
    ang = np.arange(S, dtype=np.float32)[None, :] * inv.astype(np.float32)[:, None]
    ang = np.concatenate([ang, ang], axis=0)
    sign = np.where(np.arange(ROPE) < ROPE // 2, -1.0, 1.0).astype(np.float32)[:, None]
    rope = np.stack([np.cos(ang), np.sin(ang) * sign], axis=1).astype(np.float32)
    return blob, rope


class Phase:

    def __init__(self, before, iters, slots, outs):
        self.slots, self.outs, self.iters = slots, outs, iters
        self.slot_base = [before.slot_end[s] if before else 0 for s in range(2)]
        self.out_base = [before.out_end[s] if before else 0 for s in range(2)]
        self.slot_end = [b + iters * slots.count(s) for s, b in enumerate(self.slot_base)]
        self.out_end = [b + iters * outs.count(s) for s, b in enumerate(self.out_base)]

    def n(self, i, k):
        s = self.slots[k]
        return i * self.slots.count(s) + (self.slot_base[s] + self.slots[:k].count(s))

    def o(self, i, k):
        s = self.outs[k]
        return i * self.outs.count(s) + (self.out_base[s] + self.outs[:k].count(s))


PH_LR = Phase(None, 1, [1], [1])
PH_GLA = Phase(PH_LR, HEADS, [0, 1] * 3, [0, 1] * 3)
PH_B = Phase(PH_GLA, KC, [0, 1], [0, 1])
PH_ATT = Phase(PH_B, HEADS, [0, 1, 0, 1, 0, 1, 0, 1, 0], [0, 1, 0, 1, 0, 1, 0, 1, 0, 1])
PH_A = Phase(PH_ATT, 2, [0, 1] * 3, [0, 1, None, 0, 1, None])
PH_WO = Phase(PH_A, 1, [0, 1] * 4, [None] * 8)
PH_F0 = Phase(PH_WO, 1, [0, 1] * 2, [0, 1] * 2)
FFN_LOOPS = FFN // 256 - 2
PH_F = Phase(PH_F0, FFN_LOOPS, [0, 1] * 3, [0, None, None, 1, 0, 1])
PH_F1 = Phase(PH_F, 1, [0, 1] * 4, [0, 1, 0, 1] + [None] * 4)

PAIR_ORDER = [(0, 0), (0, 1)] + [x for t in range(TT - 2) for x in ((1, t), (0, t + 2))] + [(1, TT - 2), (1, TT - 1)]
ROWS_FFN, ROWS_LAST = 8, 8 + 2 * (FFN // 256 - 1)

G_V0, G_V1, G_K, G_Q, G_R0, G_R1 = range(6)
F_G0, F_DA, F_DB, F_U0, F_G1, F_U1 = range(6)


def score_tiles():
    out = []
    for t in range(TT):
        out.append((0, t, max(0, 2 * t - 1) * P, P if t == 0 else 2 * P))
    for r in range(4):
        out.append((1, 2 * r, 3 * r * P, P))
        out.append((1, 2 * r + 1, (3 * r + 1) * P, 2 * P))
    for t in range(TT):
        out.append((2, t, t * P, P))
    return out


def prob_blocks():
    out = []
    for g, t, off, width in score_tiles():
        first = t - (width // P - 1)
        for j in range(width // P):
            out.append((g, t, first + j, off // P + j))
    return out


def token_view(ap, g, t):
    if g == 0:
        return ap[:, t * P:(t + 1) * P]
    if g == 1:
        return ap[:, (t % 2) * HALF + t // 2:(t % 2 + 1) * HALF:4]
    return ap[:, t:S:TT]


def key_view(ap, g, t, width):
    if width == P:
        return token_view(ap, g, t)
    if g == 0:
        return ap[:, (t - 1) * P:(t + 1) * P]
    return ap[:, t // 2:S:4]


def hybrid_block(nc, x, norm1_g, w_in, w_gate_lr, b_gate, gla_norm_g, w_branch_a, w_branch_b,
                 w_out, norm2_g, w_ffn_in, w_ffn_down, norm_f_g, blob, rope, out):
    x_tiles = x[0].rearrange("(t p) d -> t p d", p=P)
    out_tiles = out[0].rearrange("(t p) d -> t p d", p=P)
    win = w_in[0].rearrange("(k p) n -> p k n", p=P)
    wa = w_branch_a[0].rearrange("(k p) n -> p k n", p=P)
    wb = w_branch_b[0].rearrange("(k p) n -> p k n", p=P)
    wo = w_out[0].rearrange("(k p) n -> p k n", p=P)
    wfi = w_ffn_in[0].rearrange("(k p) n -> p k n", p=P)
    wfd = w_ffn_down[0].rearrange("(k p) n -> p k n", p=P)
    stats_dram = nc.dram_tensor("stats_dram", (S, 2 * GROUPS), F32, kind="Internal").ap()

    with ExitStack() as ctx:
        ctx.enter_context(nc.allow_non_contiguous_dma(reason="a few thousand single values"))
        base = -(-nc.sbuf_base // 64) * 64

        def sb(name, at_kb, shape, dtype=F32):
            return nc.alloc_sbuf_tensor_at(name, shape, dtype, offset=base + int(at_kb * 1024))

        def sem(name):
            return ctx.enter_context(nc.semaphore(name))

        ht_hi = sb("ht_hi", 0, [P, KC, S], F32R)
        ht_lo = sb("ht_lo", 32, [P, KC, S], F32R)
        raw = [sb(f"raw{s}", 64 + 4 * s, [P, S]) for s in range(2)]
        whi = [sb(f"whi{s}", 72 + 8 * s, [P, S], F32R) for s in range(2)]
        wlo = [sb(f"wlo{s}", 76 + 8 * s, [P, S], F32R) for s in range(2)]
        consts = sb("consts", 88, [P, C_END])
        small = sb("small", 92.75, [P, 288])
        rope_sb = sb("rope_sb", 94, [ROPE, 2, S])
        x_in = sb("x_in", 102, [P, TT, D])
        gain1 = sb("gain1", 134, [P, D])
        square1 = sb("square1", 138, [P, D])
        xn = sb("xn", 142, [P, 4, D])
        v_tok = sb("v_tok", 102, [P, TT, GV])
        turn = sb("turn", 110, [P, 2, S])
        o_tok = sb("o_tok", 110, [P, TT, GV])
        k_dec = sb("k_dec", 118, [P, S])
        q_dec = sb("q_dec", 122, [P, S])
        q_int = sb("q_int", 126, [P, S])
        k_tok = sb("k_tok", 130, [P, TT, P])
        gla_raw = sb("gla_raw", 134, [P, KC, S])
        att_t = sb("att_t", 166, [P, TT, P])
        gla_silu = sb("gla_silu", 170, [P, 2, S])
        b_cum = sb("b_cum", 178, [P, S])
        diff1 = sb("diff1", 182, [P, S])
        diff2 = sb("diff2", 186, [P, S])
        exp_a = sb("exp_a", 190, [P, S])
        exp_b = sb("exp_b", 194, [P, S])
        glr_t = sb("glr_t", 198, [2 * RANK, S])
        state = sb("state", 202, [P, 4, GV])
        square_g = sb("square_g", 206, [P, GV])
        k_cross = sb("k_cross", 94, [P, TT, CH])
        q_cross = sb("q_cross", 96, [P, TT, CH])
        mix = sb("mix", 102, [P, KC, S])
        gla_lo = sb("gla_lo", 134, [P, KC, S], F32R)
        gla_hi = sb("gla_hi", 166, [P, KC, S], F32R)
        gate_b = sb("gate_b", 198, [P, S])
        attn_raw = sb("attn_raw", 134, [P, HEADS, S])
        qkv = [sb(f"qkv{r}", 150 + 4 * r, [P, S]) for r in range(3)]
        prob = [sb("prob0", 162, [P, 15 * P]), sb("prob1", 169.5, [P, 12 * P]),
                sb("prob2", 175.5, [P, 8 * P])]
        va_tok = sb("va_tok", 179.5, [P, GROUPS, TT, HD])
        prob_t = sb("prob_t", 191.5, [P, 3, HALF])
        rotated = sb("rotated", 197.5, [ROPE, S])
        own_stats = sb("own_stats", 202, [P, GROUPS, TT, 2])
        neg_max = sb("neg_max", 202.25, [P, GROUPS, TT])
        all_stats = sb("all_stats", 202.5, [P, GROUPS, TT, 2 * GROUPS])
        top = sb("top", 203.25, [P, GROUPS * TT])
        shifted = sb("shifted", 203.5, [P, GROUPS * TT, GROUPS])
        scaled = sb("scaled", 204, [P, GROUPS * TT, GROUPS])
        total = sb("total", 204.5, [P, GROUPS * TT])
        weight = sb("weight", 204.75, [P, GROUPS, TT])
        attn_hi = sb("attn_hi", 166, [P, HEADS, S], F32R)
        attn_lo = sb("attn_lo", 182, [P, HEADS, S], F32R)
        gate_a = sb("gate_a", 198, [P, 2, S])
        mix_lo = sb("mix_lo", 102, [P, KC, S], F32R)
        mix_hi = sb("mix_hi", 134, [P, KC, S], F32R)
        x2 = sb("x2", 0, [P, TT, D])
        h2_lo = sb("h2_lo", 32, [P, KC, S], F32R)
        h2_hi = sb("h2_hi", 166, [P, KC, S], F32R)
        gain2 = sb("gain2", 94, [P, D])
        gain_f = sb("gain_f", 98, [P, D])
        xn2 = sb("xn2", 102, [P, 4, D])
        out_sb = sb("out_sb", 102, [P, 4, D])
        square2 = sb("square2", 118, [P, D])
        silu_g = sb("silu_g", 122, [P, S])
        gated = sb("gated", 126, [P, S])
        act_hi = [sb(f"act_hi{n}", 134 + 16 * n, [P, 2, S], F32R) for n in range(2)]
        act_lo = [sb(f"act_lo{n}", 142 + 16 * n, [P, 2, S], F32R) for n in range(2)]

        glr_weights = whi[1][:, 0:KC * 2 * RANK].rearrange("p (k n) -> p k n", k=KC)

        ident = consts[:, C_ID:C_ID + P]
        band = consts[:, C_BAND:C_BAND + 2 * P]
        pair = consts[:, C_PAIR:C_PAIR + P]
        gla_mask = consts[:, C_GLA:C_GLA + P]
        restart = consts[:, C_RESTART:C_END]
        eps = small[:, 0:1]
        one = small[:, 1:2]
        ss1, rms1, rstd1 = small[:, 8:16], small[:, 16:24], small[:, 24:32]
        ss2, rms2, rstd2 = small[:, 32:40], small[:, 40:48], small[:, 48:56]
        ss3, rms3, rstd3 = small[:, 56:64], small[:, 64:72], small[:, 72:80]
        ssg, rmsg, rstdg = small[:, 80:88], small[:, 88:96], small[:, 96:104]
        b_gate_sb = small[:, 104:108]
        gla_gain = small[:, 108:110]
        b_gate_head = small[:, 110:111]
        decay = small[:, 112:128]
        decay_two = small[:, 128:136]
        w_gate_head = sb("w_gate_head", 207, [2 * RANK, P])

        proj = [ctx.enter_context(nc.psum_tensor(f"proj{b}", [P, S], F32)) for b in range(2)]
        aux = ctx.enter_context(nc.psum_tensor("aux", [P, 4, HALF], F32))
        aux_a = aux[:, 0:2, :].rearrange("p a b -> p (a b)")
        aux_b = aux[:, 2:4, :].rearrange("p a b -> p (a b)")

        def output_psum(t):
            return proj[1][:, t % 2 * HALF:t % 2 * HALF + GV]

        loaded = [sem(f"loaded{s}") for s in range(2)]
        rounded = [sem(f"rounded{s}") for s in range(2)]
        split = [sem(f"split{s}") for s in range(2)]
        multiplied = [sem(f"multiplied{s}") for s in range(2)]
        out_read = [sem(f"out_read{s}") for s in range(2)]

        passed = {e.engine: sem(f"passed_{n}") for n, e in
                  (("sync", nc.sync), ("vector", nc.vector), ("gpsimd", nc.gpsimd))}
        ident_loaded = sem("ident_loaded")
        masks_loaded = sem("masks_loaded")
        gain1_loaded = sem("gain1_loaded")
        gla_gain_loaded = sem("gla_gain_loaded")
        const_set = sem("const_set")
        rope_loaded = sem("rope_loaded")
        x_loaded = [sem(f"x_loaded{t}") for t in range(TT)]
        x2_loaded = [sem(f"x2_loaded{t}") for t in range(TT)]
        gains_loaded = sem("gains_loaded")
        gain_f_loaded = sem("gain_f_loaded")
        norm_sem = [{k: sem(f"norm{n}_{k}") for k in
                     ("squared", "root", "recip", "scaled", "turned", "hi", "lo")} for n in (1, 2, 3)]

        glr_ready = sem("glr_ready")
        gate_weights_loaded = sem("gate_weights_loaded")
        z_done = sem("z_done")
        soft_step = sem("soft_step")
        soft_ready = sem("soft_ready")
        z_clamped = sem("z_clamped")
        log_a_ready = sem("log_a_ready")
        cumsum_done = sem("cumsum_done")
        diffs_ready = sem("diffs_ready")
        k_exps_ready = sem("k_exps_ready")
        q_exps_ready = sem("q_exps_ready")
        k_scaled = sem("k_scaled")
        k_read = sem("k_read")
        q_read = sem("q_read")
        cross_ready = sem("cross_ready")
        q_scaled = sem("q_scaled")
        v_read = sem("v_read")
        gla_turned = sem("gla_turned")
        gla_turn_read = sem("gla_turn_read")
        att_t_cleared = sem("att_t_cleared")
        att_t_done = sem("att_t_done")
        att_t_ready = sem("att_t_ready")
        update_done = sem("update_done")
        state_ready = sem("state_ready")
        o_done = sem("o_done")
        o_read = sem("o_read")
        gla_squared = sem("gla_squared")
        gla_root = sem("gla_root")
        gla_recip = sem("gla_recip")
        o_normed = sem("o_normed")
        o_turned = sem("o_turned")
        gate_r_ready = sem("gate_r_ready")
        gla_written = sem("gla_written")
        gla_hi_ready = sem("gla_hi_ready")
        gla_lo_ready = sem("gla_lo_ready")
        gated_b = sem("gated_b")

        qk_copied = sem("qk_copied")
        rope_step = sem("rope_step")
        qk_ready = sem("qk_ready")
        va_ready = sem("va_ready")
        va_turned = sem("va_turned")
        va_tok_ready = sem("va_tok_ready")
        scores_done = sem("scores_done")
        scores_masked = sem("scores_masked")
        neg_max_ready = sem("neg_max_ready")
        exps_done = sem("exps_done")
        stats_stored = [sem(f"stats_stored{g}") for g in range(GROUPS)]
        stats_back = [sem(f"stats_back{g}") for g in range(GROUPS)]
        combine_step = sem("combine_step")
        shift_exp_ready = sem("shift_exp_ready")
        weight_ready = sem("weight_ready")
        prob_weighted = sem("prob_weighted")
        prob_turned = sem("prob_turned")
        prob_t_ready = sem("prob_t_ready")
        pv_done = sem("pv_done")
        attn_written = sem("attn_written")
        attn_hi_ready = sem("attn_hi_ready")
        attn_lo_ready = sem("attn_lo_ready")

        branch_a_half = sem("branch_a_half")
        gate_a_step = sem("gate_a_step")
        gated_a = sem("gated_a")
        mix_hi_ready = sem("mix_hi_ready")
        mix_lo_ready = sem("mix_lo_ready")
        rows_done = sem("rows_done")
        rows_added = sem("rows_added")
        silu_ready = sem("silu_ready")
        gated_ready = sem("gated_ready")
        act_hi_ready = sem("act_hi_ready")
        act_lo_ready = sem("act_lo_ready")
        out_stored = [sem(f"out_stored{b}") for b in range(4)]

        block = ctx.enter_context(nc.Block())

        def wait_apart(eng, semaphore, value):
            eng.wait_ge(semaphore, value)
            eng.sem_inc(passed[eng.engine], 1)

        def load_unit(sp, ph, i, k, dst, src):
            s = ph.slots[k]
            wait_apart(sp, split[s], ph.n(i, k) + 1)
            sp.dma_start(dst, src).then_inc(loaded[s], 16)

        def round_unit(act, ph, i, k, cols=S):
            s = ph.slots[k]
            act.wait_ge(loaded[s], (ph.n(i, k) + 1) * 16)
            act.wait_ge(multiplied[s], ph.n(i, k) + 1)
            act.activation(whi[s][:, 0:cols], raw[s][:, 0:cols], ACT.Copy).then_inc(rounded[s], 1)

        def split_unit(dve, ph, i, k, cols=S):
            s = ph.slots[k]
            dve.wait_ge(rounded[s], ph.n(i, k) + 1)
            dve.tensor_tensor(wlo[s][:, 0:cols], raw[s][:, 0:cols], whi[s][:, 0:cols].bitcast(F32),
                              ALU.subtract).then_inc(split[s], 1)

        def slot_weights(s, k_chunks, cols):
            n = k_chunks * cols
            return (whi[s][:, 0:n].rearrange("p (k n) -> p k n", k=k_chunks),
                    wlo[s][:, 0:n].rearrange("p (k n) -> p k n", k=k_chunks))

        def three_products(pe, dst, chunks):
            last = 3 * len(chunks) - 1
            for c, (a_hi, a_lo, b_hi, b_lo) in enumerate(chunks):
                pe.matmul(dst, a_hi, b_lo, start=(c == 0), stop=False)
                pe.matmul(dst, a_lo, b_hi, start=False, stop=False)
                mm = pe.matmul(dst, a_hi, b_hi, start=False, stop=(3 * c + 2 == last))
            return mm

        def feature_half(pe, ph, i, k, hi, lo, h):
            s, o = ph.slots[k], ph.outs[k]
            w_h, w_l = slot_weights(s, KC, P)
            if h == 0:
                pe.wait_ge(split[s], ph.n(i, k) + 2)
                pe.wait_ge(out_read[o], ph.o(i, k) + 1)
            cols = slice(h * HALF, (h + 1) * HALF)
            mm = three_products(pe, proj[o][:, cols],
                                [(w_h[:, c, :], w_l[:, c, :], hi[:, c, cols], lo[:, c, cols])
                                 for c in range(KC)])
            if h == 1:
                mm.then_inc(multiplied[s], 1)

        def feature_unit(pe, ph, i, k, hi, lo):
            for h in range(2):
                feature_half(pe, ph, i, k, hi, lo, h)

        def low_rank_half(pe, h, chunks=range(KC)):
            cols = slice(h * HALF, (h + 1) * HALF)
            for c in chunks:
                for part in (ht_lo, ht_hi):
                    mm = pe.matmul(proj[1][0:2 * RANK, cols], glr_weights[:, c, :], part[:, c, cols],
                                   start=(c == 0 and part is ht_lo), stop=(c == KC - 1 and part is ht_hi))
            return mm

        def unit_multiplied(eng, ph, i, k):
            eng.wait_ge(multiplied[ph.slots[k]], ph.n(i, k) + 2)

        def row_unit(pe, ph, i, k, hi, lo, row):
            for t in range(TT):
                if ph is PH_WO and k == 0 and t % 2 == 0 and t < 4:
                    pe.wait_ge(gate_a_step, KC + 1 + t // 2)
                row_tile(pe, ph, i, k, hi, lo, t, t, row)

        def row_tile(pe, ph, i, k, hi, lo, t, j, row):
            s = ph.slots[k]
            w_h, w_l = slot_weights(s, 2, HALF)
            if t == 0:
                pe.wait_ge(split[s], ph.n(i, k) + 2)
            pe.wait_ge(rows_added, row * TT + (j + 1))
            cols = slice(t * P, (t + 1) * P)
            mm = three_products(pe, aux[:, j % 4, :],
                                [(hi[:, c, cols], lo[:, c, cols], w_h[:, c, :], w_l[:, c, :])
                                 for c in range(2)])
            mm.then_inc(*((rows_done, 1) if t < TT - 1 else (multiplied[s], 1)))

        def add_rows(dve, ph, i, k, half, row):
            for t in range(TT):
                if ph is PH_WO and k < 2:
                    dve.wait_ge(x2_loaded[t], 16)
                if t < TT - 1:
                    dve.wait_ge(rows_done, row * (TT - 1) + (t + 1))
                else:
                    unit_multiplied(dve, ph, i, k)
                dst = x2[:, t, half * HALF:(half + 1) * HALF]
                dve.tensor_tensor(dst, aux[:, t % 4, :], dst, ALU.add).then_inc(rows_added, 1)

        def add_pair_tile(dve, ph, first, j, row):
            u, t = PAIR_ORDER[j]
            if t < TT - 1:
                signalled = sum(tile < TT - 1 for _, tile in PAIR_ORDER[:j + 1])
                dve.wait_ge(rows_done, row * (TT - 1) + signalled)
            else:
                unit_multiplied(dve, ph, 0, first + u)
            dst = x2[:, t, u * HALF:(u + 1) * HALF]
            dve.tensor_tensor(dst, aux[:, j % 4, :], dst, ALU.add).then_inc(rows_added, 1)

        def pair_added(eng, t, row):
            eng.wait_ge(rows_added, 4 + row * TT + PAIR_ORDER.index((1, t)) + 1)

        def norm_root(act, n, t, src, square, ss, rms):
            sems = norm_sem[n]
            act.activation(square[:, :], src, ACT.Square, accum_out=ss[:, t:t + 1])\
               .then_inc(sems["squared"], 1)
            act.wait_ge(sems["squared"], t + 1)
            act.activation(rms[:, t:t + 1], ss[:, t:t + 1], ACT.Sqrt, bias=eps, scale=1.0 / D)\
               .then_inc(sems["root"], 1)

        def norm_scale(dve, n, t, src, rms, rstd, gain, dst):
            sems = norm_sem[n]
            dve.wait_ge(sems["root"], t + 1)
            dve.reciprocal(rstd[:, t:t + 1], rms[:, t:t + 1]).then_inc(sems["recip"], 1)
            dve.wait_ge(sems["recip"], t + 1)
            dve.scalar_tensor_tensor(dst, src, rstd[:, t:t + 1], gain[:, :], ALU.mult, ALU.mult)\
               .then_inc(sems["scaled"], 1)

        def turn_psum(n, t):
            if n == 1:
                return proj[(t + 1) % 2][:, :] if t < 5 else (aux_b, aux_a)[t % 2]
            return (aux_a, aux_b)[t % 2]

        def norm_turn(pe, n, t, src):
            sems = norm_sem[n]
            pe.wait_ge(sems["scaled"], t + 1)
            if n == 1 and t in (5, 6):
                pe.wait_ge(rows_added, 4 + ROWS_FFN * TT)
            elif t >= 2:
                pe.wait_ge(sems["lo"], t - 1)
            for c in range(KC):
                mm = pe.transpose(turn_psum(n, t)[:, c * P:(c + 1) * P], src[:, c * P:(c + 1) * P], ident)
            mm.then_inc(sems["turned"], 1)

        def norm_hi(act, n, t, hi):
            act.wait_ge(norm_sem[n]["turned"], t + 1)
            act.activation(hi[:, :, t * P:(t + 1) * P], turn_psum(n, t).rearrange("p (c q) -> p c q", c=KC),
                           ACT.Copy).then_inc(norm_sem[n]["hi"], 1)

        def norm_lo(dve, n, t, hi, lo):
            cols = slice(t * P, (t + 1) * P)
            dve.wait_ge(norm_sem[n]["hi"], t + 1)
            dve.tensor_tensor(lo[:, :, cols], turn_psum(n, t).rearrange("p (c q) -> p c q", c=KC),
                              hi[:, :, cols].bitcast(F32), ALU.subtract).then_inc(norm_sem[n]["lo"], 1)

        def feature_raw(s, k_chunks=KC, cols=P):
            return raw[s][:, 0:k_chunks * cols].rearrange("p (k n) -> p k n", k=k_chunks)

        @block.sync
        def _(sp):
            for t in range(TT):
                sp.dma_start(x_in[:, t, :], x_tiles[t]).then_inc(x_loaded[t], 16)
                if t == 0:
                    sp.dma_start(gain1[:, :], norm1_g.to_broadcast([P, D])).then_inc(gain1_loaded, 16)
                if t == 3:
                    load_unit(sp, PH_LR, 0, 0, feature_raw(1, KC, RANK), win[:, :, GLR:GLR + RANK])
            with sp.Fori(0, HEADS) as i:
                for k, col in ((G_V0, i * GV + GVC), (G_V1, i * GV + (GVC + P)), (G_K, i * P + GK),
                               (G_Q, i * P + GQ), (G_R0, i * GV + GR), (G_R1, i * GV + (GR + P))):
                    load_unit(sp, PH_GLA, i, k, feature_raw(k % 2), win[:, :, bass.ds(col, P)])
                    if k == G_V0:
                        for copy in range(2):
                            sp.dma_start(w_gate_head[copy * RANK:(copy + 1) * RANK, :],
                                         w_gate_lr[0][:, bass.ds(i * P, P)]).then_inc(gate_weights_loaded, 16)
                        sp.dma_start(b_gate_head, b_gate[0][bass.ds(i * P, P)].rearrange("(p a) -> p a", a=1))\
                          .then_inc(gate_weights_loaded, 16)
            with sp.Fori(0, KC) as i:
                load_unit(sp, PH_B, i, 0, feature_raw(0), win[:, :, bass.ds(i * P + GB, P)])
                load_unit(sp, PH_B, i, 1, feature_raw(1), wb[:, :, bass.ds(i * P, P)])
            with sp.Fori(0, HEADS) as i:
                for k in range(9):
                    g, col = (k // 2, (AQ, AK)[k % 2]) if k < 6 else (k - 6, AV)
                    load_unit(sp, PH_ATT, i, k, feature_raw(k % 2),
                              win[:, :, bass.ds(i * P + (col + g * HEADS * P), P)])
            with sp.Fori(0, 2) as i:
                for m in range(2):
                    for b in range(2):
                        load_unit(sp, PH_A, i, 3 * m + b, feature_raw((3 * m + b) % 2),
                                  win[:, :, bass.ds(i * HALF + (GA + (2 * m + b) * P), P)])
                    load_unit(sp, PH_A, i, 3 * m + 2, feature_raw((3 * m + 2) % 2, 4, 2 * P),
                              wa[:, :, bass.ds(i * HALF + 2 * m * P, 2 * P)])
            def load_w_out(k):
                load_unit(sp, PH_WO, 0, k, feature_raw(k % 2, 2, HALF),
                          wo[:, k // 2 * 2:k // 2 * 2 + 2, k % 2 * HALF:(k % 2 + 1) * HALF])

            load_w_out(0)
            load_w_out(1)
            sp.wait_ge(multiplied[PH_A.slots[4]], PH_A.n(1, 4) + 2)
            for t in range(TT):
                sp.dma_start(x2[:, t, :], x_tiles[t]).then_inc(x2_loaded[t], 16)
            for k in range(2, 8):
                load_w_out(k)

            def ffn_in(ph, i, k, part, b, up):
                load_unit(sp, ph, i, k, feature_raw(ph.slots[k]),
                          wfi[:, :, bass.ds(part * 256 + (b * P + up * FFN), P)])

            def ffn_down(ph, i, k, part, half):
                load_unit(sp, ph, i, k, feature_raw(ph.slots[k], 2, HALF),
                          wfd[:, bass.ds(part * 2, 2), half * HALF:(half + 1) * HALF])

            for k in range(4):
                ffn_in(PH_F0, 0, k, 0, k // 2, k % 2)
            with sp.Fori(0, FFN_LOOPS) as i:
                ffn_in(PH_F, i, F_G0, i + 1, 0, 0)
                ffn_down(PH_F, i, F_DA, i, 0)
                ffn_down(PH_F, i, F_DB, i, 1)
                ffn_in(PH_F, i, F_U0, i + 1, 0, 1)
                ffn_in(PH_F, i, F_G1, i + 1, 1, 0)
                ffn_in(PH_F, i, F_U1, i + 1, 1, 1)
            for k in range(4):
                ffn_in(PH_F1, 0, k, FFN_LOOPS + 1, k // 2, k % 2)
            for k in range(4, 8):
                ffn_down(PH_F1, 0, k, FFN_LOOPS + (k - 4) // 2, k % 2)
            for t in range(TT):
                sp.wait_ge(norm_sem[2]["scaled"], t + 1)
                sp.dma_start(out_tiles[t], out_sb[:, t % 4, :]).then_inc(out_stored[t % 4], 16)
            for b in range(4):
                sp.wait_ge(out_stored[b], 32)

        @block.gpsimd
        def _(pool):
            pool.memset(eps, EPS).then_inc(const_set, 1)
            pool.memset(one, 1.0).then_inc(const_set, 1)
            pool.dma_start(ident, blob[:, C_ID:C_ID + P]).then_inc(ident_loaded, 16)
            pool.dma_start(consts[:, C_BAND:C_END], blob[:, C_BAND:C_END]).then_inc(masks_loaded, 16)
            pool.dma_start(gla_gain, gla_norm_g[0].rearrange("(a p) -> p a", p=P)).then_inc(gla_gain_loaded, 16)

            natural = stats_dram.rearrange("(t p) s -> p t s", p=P)
            by4 = stats_dram.rearrange("(n p r) s -> p r n s", r=4, n=2)
            by16 = stats_dram.rearrange("(p t) s -> p t s", t=TT)
            pool.wait_ge(gla_lo_ready, KC)
            pool.dma_start(rope_sb[:, :, :], rope).then_inc(rope_loaded, 16)
            with pool.Fori(0, HEADS) as i:
                for g in range(GROUPS):
                    cols = slice(2 * g, 2 * g + 2)
                    wait_apart(pool, exps_done, i * (GROUPS * TT) + (g + 1) * TT)
                    if g == 0:
                        pool.dma_start(natural[:, :, cols], own_stats[:, 0, :, :]).then_inc(stats_stored[0], 16)
                    elif g == 1:
                        for r in range(4):
                            pool.dma_start(by4[:, r, :, cols], own_stats[:, 1, 2 * r:2 * r + 2, :])\
                                .then_inc(stats_stored[1], 16)
                    else:
                        pool.dma_start(by16[:, :, cols], own_stats[:, 2, :, :]).then_inc(stats_stored[2], 16)
                pool.wait_ge(stats_stored[0], i * 16 + 16)
                pool.wait_ge(stats_stored[1], i * 64 + 64)
                wait_apart(pool, stats_stored[2], i * 16 + 16)
                pool.dma_start(all_stats[:, 0, :, :], natural).then_inc(stats_back[0], 16)
                for r in range(4):
                    pool.dma_start(all_stats[:, 1, 2 * r:2 * r + 2, :], by4[:, r, :, :]).then_inc(stats_back[1], 16)
                pool.dma_start(all_stats[:, 2, :, :], by16).then_inc(stats_back[2], 16)
                pool.wait_ge(stats_back[0], i * 16 + 16)
                pool.wait_ge(stats_back[1], i * 64 + 64)
                pool.wait_ge(stats_back[2], i * 16 + 16)
            pool.dma_start(gain2[:, :], norm2_g.to_broadcast([P, D])).then_inc(gains_loaded, 16)
            pool.dma_start(gain_f[:, :], norm_f_g.rearrange("(a n) -> a n", a=1).to_broadcast([P, D]))\
                .then_inc(gain_f_loaded, 16)

        @block.tensor
        def _(pe):
            for s in range(2):
                pe.sem_inc(multiplied[s], 1)
            pe.wait_ge(ident_loaded, 16)
            for t in range(TT):
                norm_turn(pe, 0, t, xn[:, t % 4, :])
                if t == 5:
                    pe.wait_ge(split[1], PH_LR.n(0, 0) + 2)
                    low_rank_half(pe, 0, range(KC // 2))
                if t == 6:
                    low_rank_half(pe, 0, range(KC // 2, KC))
            pe.wait_ge(norm_sem[0]["lo"], TT)
            low_rank_half(pe, 1).then_inc(multiplied[1], 1)

            with pe.Fori(0, HEADS) as i:
                def turn_tiles(dst, src):
                    for t in range(TT):
                        mm = pe.transpose(dst[:, t * P:(t + 1) * P], src[:, t * P:(t + 1) * P], ident)
                    return mm

                feature_unit(pe, PH_GLA, i, G_V0, ht_hi, ht_lo)
                pe.wait_ge(gate_weights_loaded, i * 48 + 48)
                pe.wait_ge(glr_ready, 1)
                pe.wait_ge(gla_written, i * 2 + 1)
                for h in range(2):
                    mm = pe.matmul(aux_a[:, h * HALF:(h + 1) * HALF], w_gate_head[:, :],
                                   glr_t[:, h * HALF:(h + 1) * HALF], start=True, stop=True)
                mm.then_inc(z_done, 1)
                feature_unit(pe, PH_GLA, i, G_V1, ht_hi, ht_lo)
                pe.wait_ge(v_read, i * 2 + 1)
                turn_tiles(aux_b, turn[:, 0, :]).then_inc(gla_turned, 1)
                feature_unit(pe, PH_GLA, i, G_K, ht_hi, ht_lo)
                pe.wait_ge(v_read, i * 2 + 2)
                pe.wait_ge(gla_turn_read, i * 3 + 1)
                turn_tiles(aux_b, turn[:, 1, :]).then_inc(gla_turned, 1)
                feature_unit(pe, PH_GLA, i, G_Q, ht_hi, ht_lo)
                pe.wait_ge(k_scaled, i + 1)
                pe.wait_ge(gla_turn_read, i * 3 + 2)
                turn_tiles(aux_b, turn[:, 0, :]).then_inc(gla_turned, 1)
                feature_unit(pe, PH_GLA, i, G_R0, ht_hi, ht_lo)
                pe.wait_ge(att_t_cleared, 1)
                pe.wait_ge(q_scaled, i + 1)
                for t in range(TT):
                    cols = slice(t * P, (t + 1) * P)
                    pe.matmul(aux_a[:, cols], k_dec[:, cols], q_dec[:, cols], start=True, stop=True)
                    mm = pe.matmul(aux_a[0:CH, t * P + CH:(t + 1) * P], k_cross[:, t, :], q_cross[:, t, :],
                                   start=True, stop=True)
                mm.then_inc(att_t_done, 1)
                pe.wait_ge(gla_turn_read, i * 3 + 3)

                def update(t):
                    if t >= 2:
                        pe.wait_ge(state_ready, i * 7 + (t - 1))
                    pe.matmul(aux[:, 2 + t % 2, 0:GV], k_tok[:, t, :], v_tok[:, t, :],
                              start=True, stop=True).then_inc(update_done, 1)

                update(0)
                update(1)
                pe.wait_ge(att_t_ready, i + 1)
                for t in range(TT):
                    if t >= 2:
                        pe.wait_ge(o_read, i * TT + (t - 1))
                    mm = pe.matmul(output_psum(t), att_t[:, t, :], v_tok[:, t, :], start=True, stop=(t == 0))
                    if t:
                        pe.wait_ge(state_ready, i * 7 + t)
                        mm = pe.matmul(output_psum(t), q_int[:, t * P:(t + 1) * P], state[:, t % 4, :],
                                       start=False, stop=True)
                    mm.then_inc(o_done, 1)
                    if t + 2 < TT - 1:
                        update(t + 2)
                pe.wait_ge(o_read, i * TT + TT)
                feature_unit(pe, PH_GLA, i, G_R1, ht_hi, ht_lo)
                pe.wait_ge(o_normed, i + 1)
                for v, dst in enumerate((aux_a, aux_b)):
                    for t in range(TT):
                        mm = pe.transpose(dst[:, t * P:(t + 1) * P], o_tok[:, t, v * P:(v + 1) * P], ident)
                    mm.then_inc(o_turned, 1)

            with pe.Fori(0, KC) as i:
                feature_unit(pe, PH_B, i, 0, ht_hi, ht_lo)
                pe.wait_ge(gla_lo_ready, KC)
                feature_unit(pe, PH_B, i, 1, gla_hi, gla_lo)

            with pe.Fori(0, HEADS) as i:
                def scores(g):
                    pe.wait_ge(qk_ready, i * 6 + (2 * g + 2))
                    q, k = qkv[2 * g % 3], qkv[(2 * g + 1) % 3]
                    tiles = [x for x in score_tiles() if x[0] == g]
                    for n, (_, t, off, width) in enumerate(tiles):
                        if g == 0 and n == 0:
                            pe.wait_ge(prob_t_ready, i * 9 + 1)
                        elif g > 0 and n == 0:
                            pe.wait_ge(scores_masked, i * 24 + 8 * g)
                        pe.matmul(aux[:, n // 2, n % 2 * 2 * P:n % 2 * 2 * P + width],
                                  token_view(q, g, t), key_view(k, g, t, width),
                                  start=True, stop=True).then_inc(scores_done, 1)

                def turn_values(g, bank):
                    pe.wait_ge(va_ready, i * 3 + (g + 1))
                    for t in range(TT):
                        mm = pe.transpose(aux[:, bank + t // 4, t % 4 * P:(t % 4 + 1) * P],
                                          token_view(qkv[g], g, t), ident)
                    mm.then_inc(va_turned, 1)

                for k in range(9):
                    feature_unit(pe, PH_ATT, i, k, ht_hi, ht_lo)
                    if k in (2, 4, 6):
                        scores(k // 2 - 1)
                    if k == 7:
                        pe.wait_ge(scores_masked, i * 24 + 24)
                        turn_values(0, 0)
                turn_values(1, 2)
                pe.wait_ge(va_tok_ready, i * 3 + 1)
                turn_values(2, 0)
                blocks = prob_blocks()
                chunks = [blocks[c:c + 4] for c in range(0, len(blocks), 4)]
                started = set()

                def turn_probs(c):
                    if c < 2:
                        pe.wait_ge(va_tok_ready, i * 3 + 2)
                    elif c < 4:
                        pe.wait_ge(va_tok_ready, i * 3 + 3)
                    else:
                        pe.wait_ge(prob_t_ready, i * 9 + (c - 3 + 1))
                    if c == 0:
                        pe.wait_ge(prob_weighted, i * 24 + 24)
                    for j, (g, t, kt, col) in enumerate(chunks[c]):
                        mm = pe.transpose(aux[:, (c + 2) % 4, j * P:(j + 1) * P],
                                          prob[g][:, col * P:(col + 1) * P], ident)
                    mm.then_inc(prob_turned, 1)

                def values(c):
                    pe.wait_ge(prob_t_ready, i * 9 + (c + 1 + 1))
                    if c == 0:
                        pe.wait_ge(out_read[1], PH_ATT.o(i, 9) + 1)
                    for j, (g, t, kt, col) in enumerate(chunks[c]):
                        dst = token_view(proj[1], g, t)
                        src = prob_t[:, c % 3, j * P:(j + 1) * P]
                        parts = [(dst, src)]
                        if g == 2:
                            parts = [(dst[:, 64 * b:64 * b + 64], src[:, 64 * b:64 * b + 64]) for b in range(2)]
                        for b, (d, r) in enumerate(parts):
                            bank = b if g == 2 else (t // 4 if g == 0 else t % 2)
                            mm = pe.matmul(d, va_tok[:, g, kt, :], r, start=bank not in started,
                                           stop=True, skip_group_check=True)
                            started.add(bank)
                    return mm

                for c in range(len(chunks) + 2):
                    if c < len(chunks):
                        turn_probs(c)
                    if c >= 2:
                        mm = values(c - 2)
                mm.then_inc(pv_done, 1)

            with pe.Fori(0, 2) as i:
                for m in range(2):
                    for b in range(2):
                        feature_unit(pe, PH_A, i, 3 * m + b, ht_hi, ht_lo)
                    k = 3 * m + 2
                    w_h, w_l = slot_weights(PH_A.slots[k], 4, 2 * P)
                    pe.wait_ge(split[PH_A.slots[k]], PH_A.n(i, k) + 2)
                    pe.wait_ge(attn_lo_ready, HEADS)
                    for b in range(2):
                        pe.wait_ge(gate_a_step, i * 4 + (2 * m + b + 1))
                        for h in range(2):
                            cols = slice(h * HALF, (h + 1) * HALF)
                            feats = slice(b * P, (b + 1) * P)
                            mm = three_products(pe, aux[:, 2 * b + h, :],
                                                [(w_h[:, c, feats], w_l[:, c, feats],
                                                  attn_hi[:, c, cols], attn_lo[:, c, cols])
                                                 for c in range(HEADS)])
                        mm.then_inc(*((branch_a_half, 1) if b == 0 else (multiplied[PH_A.slots[k]], 1)))

            for k in range(6):
                p = k // 2
                pe.wait_ge(mix_lo_ready, 2 * p + 2)
                row_unit(pe, PH_WO, 0, k, mix_hi[:, 2 * p:2 * p + 2, :], mix_lo[:, 2 * p:2 * p + 2, :], k)
            pe.wait_ge(mix_lo_ready, KC)
            for j, (u, t) in enumerate(PAIR_ORDER):
                row_tile(pe, PH_WO, 0, 6 + u, mix_hi[:, 6:8, :], mix_lo[:, 6:8, :], t, j, 6)
                if u == 1 and t >= 2:
                    norm_turn(pe, 1, t - 2, xn2[:, (t - 2) % 4, :])

            pe.wait_ge(norm_sem[1]["lo"], 4)
            feature_half(pe, PH_F0, 0, 0, h2_hi, h2_lo, 0)
            norm_turn(pe, 1, 6, xn2[:, 2, :])
            norm_turn(pe, 1, 7, xn2[:, 3, :])
            feature_half(pe, PH_F0, 0, 1, h2_hi, h2_lo, 0)
            pe.wait_ge(norm_sem[1]["lo"], TT)
            feature_half(pe, PH_F0, 0, 0, h2_hi, h2_lo, 1)
            feature_half(pe, PH_F0, 0, 1, h2_hi, h2_lo, 1)
            for k in range(2, 4):
                feature_unit(pe, PH_F0, 0, k, h2_hi, h2_lo)
            with pe.Fori(0, FFN_LOOPS) as i:
                feature_unit(pe, PH_F, i, F_G0, h2_hi, h2_lo)
                pe.wait_ge(act_lo_ready, i * 2 + 2)
                row_unit(pe, PH_F, i, F_DA, act_hi[0], act_lo[0], i * 2 + ROWS_FFN)
                row_unit(pe, PH_F, i, F_DB, act_hi[0], act_lo[0], i * 2 + (ROWS_FFN + 1))
                feature_unit(pe, PH_F, i, F_U0, h2_hi, h2_lo)
                feature_unit(pe, PH_F, i, F_G1, h2_hi, h2_lo)
                feature_unit(pe, PH_F, i, F_U1, h2_hi, h2_lo)
            for k in range(4):
                feature_unit(pe, PH_F1, 0, k, h2_hi, h2_lo)
            for k in range(4, 6):
                row_unit(pe, PH_F1, 0, k, act_hi[0], act_lo[0], ROWS_LAST - 2 + (k - 4))
            pe.wait_ge(act_lo_ready, 2 * FFN_LOOPS + 4)
            for j, (u, t) in enumerate(PAIR_ORDER):
                row_tile(pe, PH_F1, 0, 6 + u, act_hi[1], act_lo[1], t, j, ROWS_LAST)

        @block.scalar
        def _(act):
            for b in range(2):
                act.sem_inc(out_read[b], 1)
            act.wait_ge(const_set, 2)
            act.activation(small[:, 2:3], eps, ACT.Sqrt, bias=eps)
            for t in range(TT + 2):
                if t < TT:
                    act.wait_ge(x_loaded[t], 16)
                    norm_root(act, 0, t, x_in[:, t, :], square1, ss1, rms1)
                if t >= 2:
                    norm_hi(act, 0, t - 2, ht_hi)
                if t == 2:
                    act.wait_ge(loaded[1], 16)
                    act.activation(glr_weights[:, :, 0:RANK], feature_raw(1, KC, RANK), ACT.Copy)\
                       .then_inc(rounded[1], 1)
            round_unit(act, PH_GLA, 0, 0)
            unit_multiplied(act, PH_LR, 0, 0)
            act.activation(glr_t[:, :], proj[1][0:2 * RANK, :], ACT.Copy).then_inc(glr_ready, 1)
            act.wait_ge(glr_ready, 1)
            act.sem_inc(out_read[1], 1)
            round_unit(act, PH_GLA, 0, 1)

            with act.Fori(0, HEADS) as i:
                def round_next(k):
                    if k + 2 < 6:
                        round_unit(act, PH_GLA, i, k + 2)
                    else:
                        round_unit(act, PH_GLA, i + 1, k - 4)

                def done(k):
                    unit_multiplied(act, PH_GLA, i, k)

                round_next(G_V0)
                done(G_V0)
                act.activation(turn[:, 0, :], proj[0][:, :], ACT.Copy).then_inc(v_read, 1)
                act.wait_ge(v_read, i * 2 + 1)
                act.sem_inc(out_read[0], 1)
                act.wait_ge(z_done, i + 1)
                act.activation(diff1[:, :], aux_a, ACT.Abs, bias=b_gate_head).then_inc(soft_step, 1)
                act.wait_ge(soft_step, i * 2 + 1)
                act.activation(diff1[:, :], diff1[:, :], ACT.Exp, scale=-1.0).then_inc(soft_step, 1)
                act.wait_ge(soft_step, i * 2 + 2)
                act.activation(diff1[:, :], diff1[:, :], ACT.Ln, bias=one).then_inc(soft_ready, 1)
                round_next(G_V1)
                done(G_V1)
                act.activation(turn[:, 1, :], proj[1][:, :], ACT.Copy).then_inc(v_read, 1)
                act.wait_ge(v_read, i * 2 + 2)
                act.sem_inc(out_read[1], 1)
                act.wait_ge(gla_turned, i * 3 + 1)
                act.activation(v_tok[:, :, 0:P], aux_b.rearrange("p (t n) -> p t n", t=TT), ACT.Copy)\
                   .then_inc(gla_turn_read, 1)
                act.wait_ge(diffs_ready, i + 1)
                act.activation(exp_a[:, :], diff1[:, :], ACT.Exp, scale=-1.0 / GATE_NORM)
                act.activation(exp_b[:, :], diff2[:, :], ACT.Exp, scale=1.0 / GATE_NORM)
                act.activation(decay, b_cum[:, CH - 1:S:CH], ACT.Exp, scale=1.0 / GATE_NORM)\
                   .then_inc(k_exps_ready, 1)
                round_next(G_K)
                act.wait_ge(gla_turned, i * 3 + 2)
                act.activation(v_tok[:, :, P:2 * P], aux_b.rearrange("p (t n) -> p t n", t=TT), ACT.Copy)\
                   .then_inc(gla_turn_read, 1)
                act.wait_ge(k_scaled, i + 1)
                act.activation(exp_a[:, :], diff1[:, :], ACT.Exp, scale=1.0 / GATE_NORM)
                act.activation(exp_b[:, :], b_cum[:, :], ACT.Exp, scale=1.0 / GATE_NORM)\
                   .then_inc(q_exps_ready, 1)
                round_next(G_Q)
                act.wait_ge(gla_turned, i * 3 + 3)
                act.activation(k_tok[:, :, :], aux_b.rearrange("p (t n) -> p t n", t=TT), ACT.Copy)\
                   .then_inc(gla_turn_read, 1)
                round_next(G_R0)
                done(G_R0)
                act.activation(gla_silu[:, 0, :], proj[0][:, :], ACT.Silu).then_inc(gate_r_ready, 1)
                act.wait_ge(gate_r_ready, i * 2 + 1)
                act.sem_inc(out_read[0], 1)
                for t in range(TT):
                    act.wait_ge(o_done, i * TT + (t + 1))
                    if t:
                        act.wait_ge(gla_squared, i * TT + t)
                    act.activation(square_g[:, :], output_psum(t), ACT.Square,
                                   accum_out=ssg[:, t:t + 1]).then_inc(gla_squared, 1)
                    act.activation(o_tok[:, t, :], output_psum(t), ACT.Copy).then_inc(o_read, 1)
                act.wait_ge(gla_squared, i * TT + TT)
                act.activation(rmsg, ssg, ACT.Sqrt, bias=eps, scale=1.0 / GV).then_inc(gla_root, 1)
                round_next(G_R1)
                done(G_R1)
                act.activation(gla_silu[:, 1, :], proj[1][:, :], ACT.Silu).then_inc(gate_r_ready, 1)
                act.wait_ge(gate_r_ready, i * 2 + 2)
                act.sem_inc(out_read[1], 1)

            act.wait_ge(gla_written, 2 * HEADS + 1)
            for c in range(KC):
                act.activation(gla_hi[:, c, :], gla_raw[:, c, :], ACT.Copy).then_inc(gla_hi_ready, 1)
            with act.Fori(0, KC) as i:
                round_unit(act, PH_B, i + 1, 0)
                unit_multiplied(act, PH_B, i, 0)
                act.wait_ge(out_read[1], PH_B.o(i, 1) + 1)
                act.activation(gate_b[:, :], proj[0][:, :], ACT.Sigmoid).then_inc(out_read[0], 1)
                round_unit(act, PH_B, i + 1, 1)

            with act.Fori(0, HEADS) as i:
                def round_next(k):
                    if k + 2 < 9:
                        round_unit(act, PH_ATT, i, k + 2)
                    elif k == 8:
                        round_unit(act, PH_ATT, i + 1, 0)
                        round_unit(act, PH_ATT, i + 1, 1)

                def exps(g):
                    act.wait_ge(neg_max_ready, i * 3 + (g + 1))
                    for t, (_, tile, off, width) in enumerate([x for x in score_tiles() if x[0] == g]):
                        part = prob[g][:, off:off + width]
                        act.activation(part, part, ACT.Exp, bias=neg_max[:, g, tile:tile + 1],
                                       scale=HD ** -0.5, accum_out=own_stats[:, g, tile, 1:2])\
                           .then_inc(exps_done, 1)

                def copy_values(g):
                    act.wait_ge(va_turned, i * 3 + (g + 1))
                    bank = (0, 2, 0)[g]
                    act.activation(va_tok[:, g, :, :], aux[:, bank:bank + 2, :].rearrange(
                        "p a (t n) -> p (a t) n", n=HD), ACT.Copy).then_inc(va_tok_ready, 1)

                for k in range(9):
                    round_next(k)
                    if k == 7:
                        exps(2)
                    unit_multiplied(act, PH_ATT, i, k)
                    if k < 6:
                        act.activation(qkv[k % 3][:, :], proj[k % 2][:, :], ACT.Copy).then_inc(qk_copied, 1)
                        if k in (3, 5):
                            exps(k // 2 - 1)
                    else:
                        act.activation(qkv[k - 6][:, :], proj[k % 2][:, :], ACT.Copy).then_inc(va_ready, 1)
                        act.wait_ge(va_ready, i * 3 + (k - 5))
                        act.sem_inc(out_read[k % 2], 1)
                        if k == 7:
                            copy_values(0)
                            act.wait_ge(combine_step, i * 5 + 2)
                            act.activation(scaled[:, :, :], shifted[:, :, :], ACT.Exp, scale=HD ** -0.5)\
                               .then_inc(shift_exp_ready, 1)
                copy_values(1)
                copy_values(2)
                for c in range(9):
                    act.wait_ge(prob_turned, i * 9 + (c + 1))
                    n = min(4, len(prob_blocks()) - 4 * c) * P
                    act.activation(prob_t[:, c % 3, 0:n], aux[:, (c + 2) % 4, 0:n], ACT.Copy)\
                       .then_inc(prob_t_ready, 1)
                act.wait_ge(pv_done, i + 1)
                act.activation(attn_raw[:, bass.ds(i, 1), :], proj[1][:, :].rearrange("p (a s) -> p a s", a=1),
                               ACT.Copy).then_inc(attn_written, 1)
                act.wait_ge(attn_written, i + 1)
                act.sem_inc(out_read[1], 1)

            for c in range(HEADS):
                act.activation(attn_hi[:, c, :], attn_raw[:, c, :], ACT.Copy).then_inc(attn_hi_ready, 1)
            with act.Fori(0, 2) as i:
                def mix_hi_block(m, b):
                    act.wait_ge(gated_a, i * 4 + (2 * m + b + 3))
                    act.activation(mix_hi[:, bass.ds(i * 4 + (2 * m + b), 1), :],
                                   mix[:, bass.ds(i * 4 + (2 * m + b), 1), :], ACT.Copy)\
                       .then_inc(mix_hi_ready, 1)

                for k in range(6):
                    if k % 3 == 2:
                        mix_hi_block(k // 3, 0)
                    if k < 4:
                        round_unit(act, PH_A, i, k + 2)
                    else:
                        round_unit(act, PH_A, i + 1, k - 4)
                    if k % 3 == 2:
                        mix_hi_block(k // 3, 1)
                    if k % 3 < 2:
                        unit_multiplied(act, PH_A, i, k)
                        act.wait_ge(gated_a, i * 4 + (k // 3 * 2 + k % 3 + 1))
                        act.activation(gate_a[:, k % 3, :], proj[PH_A.outs[k]][:, :], ACT.Sigmoid)\
                           .then_inc(out_read[PH_A.outs[k]], 1)

            for k in range(6):
                round_unit(act, PH_WO, 0, k + 2)
            for t in range(TT + 2):
                if t == TT - 1:
                    round_unit(act, PH_F0, 0, 0)
                if t < TT:
                    pair_added(act, t, 6)
                    norm_root(act, 1, t, x2[:, t, :], square2, ss2, rms2)
                if t >= 2:
                    norm_hi(act, 1, t - 2, h2_hi)
                if t == TT - 1:
                    round_unit(act, PH_F0, 0, 1)

            def silu(ph, i, k, part_use):
                unit_multiplied(act, ph, i, k)
                act.wait_ge(gated_ready, part_use)
                act.activation(silu_g[:, :], proj[0][:, :], ACT.Silu).then_inc(out_read[0], 1)

            def act_hi_block(count, b, place=0):
                act.wait_ge(gated_ready, count + 1)
                act.activation(act_hi[place][:, b, :], gated[:, :], ACT.Copy).then_inc(act_hi_ready, 1)

            for k in range(4):
                if k < 2:
                    round_unit(act, PH_F0, 0, k + 2)
                else:
                    round_unit(act, PH_F, 0, k - 2)
                if k % 2 == 0:
                    silu(PH_F0, 0, k, k // 2 + 1)
                else:
                    act_hi_block(k // 2 + 1, k // 2)
            with act.Fori(0, FFN_LOOPS) as i:
                round_unit(act, PH_F, i, F_DB)
                silu(PH_F, i, F_G0, i * 2 + 3)
                round_unit(act, PH_F, i, F_U0)
                round_unit(act, PH_F, i, F_G1)
                round_unit(act, PH_F, i, F_U1)
                act_hi_block(i * 2 + 3, 0)
                round_unit(act, PH_F, i + 1, 0)
                silu(PH_F, i, F_G1, i * 2 + 4)
                round_unit(act, PH_F, i + 1, 1)
                act_hi_block(i * 2 + 4, 1)
            for k in range(4):
                round_unit(act, PH_F1, 0, k + 2)
                if k % 2 == 0:
                    silu(PH_F1, 0, k, 2 * FFN_LOOPS + 3 + k // 2)
                else:
                    act_hi_block(2 * FFN_LOOPS + 3 + k // 2, k // 2, 1)
            for k in range(6, 8):
                round_unit(act, PH_F1, 0, k)
            for t in range(TT):
                pair_added(act, t, ROWS_LAST)
                norm_root(act, 2, t, x2[:, t, :], square2, ss3, rms3)

        @block.vector
        def _(dve):
            for s in range(2):
                dve.sem_inc(split[s], 1)
            dve.sem_inc(rows_added, 4)
            dve.sem_inc(gla_written, 1)
            dve.sem_inc(prob_t_ready, 1)
            dve.sem_inc(gated_ready, 1)
            dve.sem_inc(gate_a_step, 2)
            dve.sem_inc(gated_a, 2)
            dve.wait_ge(gain1_loaded, 16)
            for t in range(TT + 2):
                if t < TT:
                    if t >= 4:
                        dve.wait_ge(norm_sem[0]["turned"], t - 3)
                    norm_scale(dve, 0, t, x_in[:, t, :], rms1, rstd1, gain1, xn[:, t % 4, :])
                if t >= 2:
                    norm_lo(dve, 0, t - 2, ht_hi, ht_lo)
                if t == 3:
                    dve.wait_ge(rounded[1], 1)
                    dve.tensor_tensor(glr_weights[:, :, RANK:2 * RANK], feature_raw(1, KC, RANK),
                                      glr_weights[:, :, 0:RANK].bitcast(F32), ALU.subtract)\
                       .then_inc(split[1], 1)
            split_unit(dve, PH_GLA, 0, 0)
            dve.wait_ge(masks_loaded, 16)
            dve.wait_ge(gla_gain_loaded, 16)
            dve.memset(att_t[:, :, :], 0.0).then_inc(att_t_cleared, 1)
            split_unit(dve, PH_GLA, 0, 1)

            with dve.Fori(0, HEADS) as i:
                def split_next(k):
                    if k + 2 < 6:
                        split_unit(dve, PH_GLA, i, k + 2)
                    else:
                        split_unit(dve, PH_GLA, i + 1, k - 4)

                chunks = b_cum[:, :].rearrange("p (c j) -> p c j", j=CH)
                d1 = diff1[:, :].rearrange("p (c j) -> p c j", j=CH)
                d2 = diff2[:, :].rearrange("p (c j) -> p c j", j=CH)
                wide = [P, S // CH, CH]

                def by_chunk(ap):
                    return ap[:, :].rearrange("p (t c j) -> p t c j", c=2, j=CH)

                split_next(G_V0)
                dve.wait_ge(soft_step, i * 2 + 1)
                dve.tensor_scalar(diff2[:, :], aux_a, b_gate_head, 0.0, ALU.add, ALU.min)\
                   .then_inc(z_clamped, 1)
                dve.wait_ge(z_clamped, i + 1)
                dve.wait_ge(soft_ready, i + 1)
                dve.tensor_tensor(diff2[:, :], diff2[:, :], diff1[:, :], ALU.subtract).then_inc(log_a_ready, 1)
                dve.wait_ge(log_a_ready, i + 1)
                for h in range(2):
                    cols = slice(h * HALF, (h + 1) * HALF)
                    dve.tensor_tensor_scan(b_cum[:, cols], restart, diff2[:, cols], 0.0, ALU.mult, ALU.add)\
                       .then_inc(cumsum_done, 1)
                dve.wait_ge(cumsum_done, i * 2 + 2)
                dve.tensor_tensor(d1, chunks, chunks[:, :, CH // 2:CH // 2 + 1].to_broadcast(wide), ALU.subtract)
                dve.tensor_tensor(d2, chunks[:, :, CH - 1:CH].to_broadcast(wide), chunks, ALU.subtract)\
                   .then_inc(diffs_ready, 1)
                split_next(G_V1)
                split_next(G_K)
                unit_multiplied(dve, PH_GLA, i, G_K)
                dve.wait_ge(k_exps_ready, i + 1)
                dve.wait_ge(gla_turned, i * 3 + 1)
                k_ps, k_end, e_b = by_chunk(proj[0]), by_chunk(turn[:, 0, :]), by_chunk(exp_b)
                half = [P, TT, CH]
                dve.tensor_tensor(decay_two, decay[:, 0:16:2], decay[:, 1:16:2], ALU.mult)
                dve.tensor_tensor(k_cross[:, :, :], k_ps[:, :, 0, :], e_b[:, :, 0, :], ALU.mult)\
                   .then_inc(cross_ready, 1)
                dve.tensor_tensor(k_end[:, :, 1, :], k_ps[:, :, 1, :], e_b[:, :, 1, :], ALU.mult)
                dve.tensor_tensor(k_dec[:, :], proj[0][:, :], exp_a[:, :], ALU.mult).then_inc(k_read, 1)
                dve.wait_ge(k_read, i + 1)
                dve.sem_inc(out_read[0], 1)
                dve.wait_ge(cross_ready, i + 1)
                dve.tensor_tensor(k_end[:, :, 0, :], k_cross[:, :, :],
                                  decay[:, 1:16:2].rearrange("p (t a) -> p t a", a=1).to_broadcast(half),
                                  ALU.mult).then_inc(k_scaled, 1)
                split_next(G_Q)
                unit_multiplied(dve, PH_GLA, i, G_Q)
                dve.wait_ge(q_exps_ready, i + 1)
                q_ps, q_start = by_chunk(proj[1]), by_chunk(q_int)
                for dst, src, e in ((q_cross[:, :, :], q_ps[:, :, 1, :], e_b[:, :, 1, :]),
                                    (q_start[:, :, 0, :], q_ps[:, :, 0, :], e_b[:, :, 0, :]),
                                    (q_dec[:, :], proj[1][:, :], exp_a[:, :])):
                    dve.scalar_tensor_tensor(dst, src, float(P) ** -0.5, e, ALU.mult, ALU.mult)\
                       .then_inc(q_read, 1)
                dve.wait_ge(q_read, i * 3 + 3)
                dve.sem_inc(out_read[1], 1)
                dve.tensor_tensor(q_start[:, :, 1, :], q_cross[:, :, :],
                                  decay[:, 0:16:2].rearrange("p (t a) -> p t a", a=1).to_broadcast(half),
                                  ALU.mult).then_inc(q_scaled, 1)
                split_next(G_R0)
                wait_apart(dve, att_t_done, i + 1)
                dve.copy_predicated(att_t[:, :, :], gla_mask.bitcast(I32).rearrange("p (a n) -> p a n", a=1)
                                    .to_broadcast([P, TT, P]), aux_a.rearrange("p (t n) -> p t n", t=TT))\
                   .then_inc(att_t_ready, 1)
                for t in range(TT - 1):
                    dve.wait_ge(update_done, i * 7 + (t + 1))
                    if t >= 3:
                        dve.wait_ge(o_done, i * TT + (t - 2))
                    new, upd = state[:, (t + 1) % 4, :], aux[:, 2 + t % 2, 0:GV]
                    if t == 0:
                        dve.tensor_copy(new, upd).then_inc(state_ready, 1)
                    else:
                        dve.wait_ge(state_ready, i * 7 + t)
                        dve.scalar_tensor_tensor(new, state[:, t % 4, :], decay_two[:, t:t + 1], upd,
                                                 ALU.mult, ALU.add).then_inc(state_ready, 1)
                dve.wait_ge(gla_root, i + 1)
                dve.reciprocal(rstdg, rmsg).then_inc(gla_recip, 1)
                dve.wait_ge(gla_recip, i + 1)
                dve.tensor_tensor(o_tok[:, :, :], o_tok[:, :, :],
                                  rstdg.rearrange("p (t a) -> p t a", a=1).to_broadcast([P, TT, GV]),
                                  ALU.mult).then_inc(o_normed, 1)
                split_next(G_R1)
                for v, src in enumerate((aux_a, aux_b)):
                    dve.wait_ge(o_turned, i * 2 + (v + 1))
                    dve.wait_ge(gate_r_ready, i * 2 + (v + 1))
                    dve.scalar_tensor_tensor(gla_raw[:, bass.ds(i * 2 + v, 1), :],
                                             src.rearrange("p (a s) -> p a s", a=1), gla_gain[:, v:v + 1],
                                             gla_silu[:, v:v + 1, :], ALU.mult, ALU.mult)\
                       .then_inc(gla_written, 1)

            for c in range(KC):
                dve.wait_ge(gla_hi_ready, c + 1)
                dve.tensor_tensor(gla_lo[:, c, :], gla_raw[:, c, :], gla_hi[:, c, :].bitcast(F32),
                                  ALU.subtract).then_inc(gla_lo_ready, 1)
            with dve.Fori(0, KC) as i:
                split_unit(dve, PH_B, i + 1, 0)
                split_unit(dve, PH_B, i + 1, 1)
                dve.wait_ge(out_read[0], PH_B.o(i, 0) + 2)
                dve.tensor_tensor(mix[:, bass.ds(i, 1), :], proj[1][:, :].rearrange("p (a s) -> p a s", a=1),
                                  gate_b[:, :].rearrange("p (a s) -> p a s", a=1), ALU.mult)\
                   .then_inc(out_read[1], 1)

            dve.wait_ge(out_read[1], PH_B.out_end[1] + 1)
            dve.wait_ge(rope_loaded, 16)
            swap = list(range(16, 32)) + list(range(16))
            with dve.Fori(0, HEADS) as i:
                def split_next(k):
                    if k + 2 < 9:
                        split_unit(dve, PH_ATT, i, k + 2)
                    elif k == 8:
                        split_unit(dve, PH_ATT, i + 1, 0)
                        split_unit(dve, PH_ATT, i + 1, 1)

                def rotate(k):
                    src, dst = proj[k % 2][0:ROPE, :], qkv[k % 3][0:ROPE, :]
                    wait_apart(dve, qk_copied, i * 6 + (k + 1))
                    if k:
                        wait_apart(dve, qk_ready, i * 6 + k)
                    dve.stream_shuffle(rotated[:, :], src, swap).then_inc(rope_step, 1)
                    dve.wait_ge(rope_step, i * 18 + (3 * k + 1))
                    dve.tensor_tensor(rotated[:, :], rotated[:, :], rope_sb[:, 1, :], ALU.mult)\
                       .then_inc(rope_step, 1)
                    dve.tensor_tensor(dst, src, rope_sb[:, 0, :], ALU.mult).then_inc(rope_step, 1)
                    dve.wait_ge(rope_step, i * 18 + (3 * k + 3))
                    dve.sem_inc(out_read[k % 2], 1)
                    dve.tensor_tensor(dst, dst, rotated[:, :], ALU.add).then_inc(qk_ready, 1)

                def mask_scores(g):
                    for n, (_, t, off, width) in enumerate([x for x in score_tiles() if x[0] == g]):
                        wait_apart(dve, scores_done, i * 24 + (8 * g + n // 2 * 2 + 2))
                        mask = pair if g == 2 else band[:, 2 * P - width:2 * P]
                        dve.tensor_tensor_reduce(prob[g][:, off:off + width],
                                                 aux[:, n // 2, n % 2 * 2 * P:n % 2 * 2 * P + width], mask,
                                                 1.0, -3.0e38, ALU.add, ALU.max,
                                                 own_stats[:, g, t, 0:1]).then_inc(scores_masked, 1)
                    dve.wait_ge(scores_masked, i * 24 + (8 * g + 8))
                    dve.tensor_scalar(neg_max[:, g, :], own_stats[:, g, :, 0], -(HD ** -0.5), None, ALU.mult)\
                       .then_inc(neg_max_ready, 1)

                for k in range(9):
                    split_next(k)
                    if k < 6:
                        rotate(k)
                    if k in (2, 4, 6):
                        mask_scores(k // 2 - 1)
                    if k == 7:
                        for g in range(GROUPS):
                            dve.wait_ge(stats_back[g], i * (16, 64, 16)[g] + (16, 64, 16)[g])
                        every = all_stats[:, :, :, :].rearrange("p y t (g s) -> p (y t) g s", s=2)
                        dve.tensor_reduce(top[:, :], every[:, :, :, 0], AX.X, ALU.max).then_inc(combine_step, 1)
                        dve.wait_ge(combine_step, i * 5 + 1)
                        dve.tensor_tensor(shifted[:, :, :], every[:, :, :, 0],
                                          top[:, :].rearrange("p (y a) -> p y a", a=1)
                                          .to_broadcast([P, GROUPS * TT, GROUPS]), ALU.subtract)\
                           .then_inc(combine_step, 1)
                        dve.wait_ge(shift_exp_ready, i + 1)
                        dve.tensor_tensor(shifted[:, :, :], scaled[:, :, :], every[:, :, :, 1], ALU.mult)\
                           .then_inc(combine_step, 1)
                        dve.wait_ge(combine_step, i * 5 + 3)
                        dve.tensor_reduce(total[:, :], shifted[:, :, :], AX.X, ALU.add).then_inc(combine_step, 1)
                        dve.wait_ge(combine_step, i * 5 + 4)
                        dve.reciprocal(top[:, :], total[:, :]).then_inc(combine_step, 1)
                        dve.wait_ge(combine_step, i * 5 + 5)
                        own = scaled[:, :, :].rearrange("p (y t) g -> p y t g", y=GROUPS)
                        for g in range(GROUPS):
                            dve.tensor_tensor(weight[:, g, :], own[:, g, :, g], top[:, g * TT:(g + 1) * TT],
                                              ALU.mult).then_inc(weight_ready, 1)
                        for n, (g, t, off, width) in enumerate(score_tiles()):
                            if t == 0 and g < 3 and n % 8 == 0:
                                dve.wait_ge(weight_ready, i * 3 + (g + 1))
                            part = prob[g][:, off:off + width]
                            dve.tensor_scalar(part, part, weight[:, g, t:t + 1], None, ALU.mult)\
                               .then_inc(prob_weighted, 1)

            for c in range(HEADS):
                dve.wait_ge(attn_hi_ready, c + 1)
                dve.tensor_tensor(attn_lo[:, c, :], attn_raw[:, c, :], attn_hi[:, c, :].bitcast(F32),
                                  ALU.subtract).then_inc(attn_lo_ready, 1)
            with dve.Fori(0, 2) as i:
                def gate_block(m, b):
                    k = 3 * m + b
                    dve.wait_ge(out_read[PH_A.outs[k]], PH_A.o(i, k) + 2)
                    gate = gate_a[:, b:b + 1, :]
                    dve.tensor_tensor(gate, aux[:, 2 * b:2 * b + 2, :].rearrange("p (a h) s -> p a (h s)", a=1),
                                      gate, ALU.mult).then_inc(gate_a_step, 1)
                    dve.wait_ge(gate_a_step, i * 4 + (2 * m + b + 3))
                    dst = mix[:, bass.ds(i * 4 + (2 * m + b), 1), :]
                    dve.tensor_tensor(dst, dst, gate, ALU.add).then_inc(gated_a, 1)

                for k in range(6):
                    m = k // 3
                    if k % 3 == 2:
                        dve.wait_ge(branch_a_half, i * 2 + (m + 1))
                        gate_block(m, 0)
                        unit_multiplied(dve, PH_A, i, k)
                        gate_block(m, 1)
                    if k < 4:
                        split_unit(dve, PH_A, i, k + 2)
                    else:
                        split_unit(dve, PH_A, i + 1, k - 4)
                    if k % 3 == 2:
                        for b in range(2):
                            block_at = bass.ds(i * 4 + (2 * m + b), 1)
                            dve.wait_ge(mix_hi_ready, i * 4 + (2 * m + b + 1))
                            dve.tensor_tensor(mix_lo[:, block_at, :], mix[:, block_at, :],
                                              mix_hi[:, block_at, :].bitcast(F32), ALU.subtract)\
                               .then_inc(mix_lo_ready, 1)

            for k in range(6):
                add_rows(dve, PH_WO, 0, k, k % 2, k)
                split_unit(dve, PH_WO, 0, k + 2)
            dve.wait_ge(gains_loaded, 16)

            def scale2(t):
                if t >= 4:
                    dve.wait_ge(norm_sem[1]["turned"], t - 3)
                norm_scale(dve, 1, t, x2[:, t, :], rms2, rstd2, gain2, xn2[:, t % 4, :])

            for j, (u, t) in enumerate(PAIR_ORDER):
                add_pair_tile(dve, PH_WO, 6, j, 6)
                if u == 1 and t >= 1:
                    scale2(t - 1)
                if u == 1 and t >= 3:
                    norm_lo(dve, 1, t - 3, h2_hi, h2_lo)
                if (u, t) == (1, TT - 2):
                    split_unit(dve, PH_F0, 0, 0)
            scale2(TT - 1)
            for t in range(TT - 3, TT):
                norm_lo(dve, 1, t, h2_hi, h2_lo)
                if t == TT - 3:
                    split_unit(dve, PH_F0, 0, 1)

            def hidden(ph, i, k, count, b, place=0):
                if not isinstance(count, int) or count > 1:
                    dve.wait_ge(act_lo_ready, count - 1)
                unit_multiplied(dve, ph, i, k)
                dve.wait_ge(out_read[0], ph.o(i, k - (3 if ph is PH_F and k == F_U0 else 1)) + 2)
                dve.tensor_tensor(gated[:, :], proj[1][:, :], silu_g[:, :], ALU.mult).then_inc(gated_ready, 1)
                dve.wait_ge(gated_ready, count + 1)
                dve.sem_inc(out_read[1], 1)
                dve.wait_ge(act_hi_ready, count)
                dve.tensor_tensor(act_lo[place][:, b, :], gated[:, :], act_hi[place][:, b, :].bitcast(F32), ALU.subtract)\
                   .then_inc(act_lo_ready, 1)

            for k in range(4):
                if k < 2:
                    split_unit(dve, PH_F0, 0, k + 2)
                else:
                    split_unit(dve, PH_F, 0, k - 2)
                if k % 2:
                    hidden(PH_F0, 0, k, k // 2 + 1, k // 2)
            with dve.Fori(0, FFN_LOOPS) as i:
                split_unit(dve, PH_F, i, F_DB)
                add_rows(dve, PH_F, i, F_DA, 0, i * 2 + ROWS_FFN)
                split_unit(dve, PH_F, i, F_U0)
                add_rows(dve, PH_F, i, F_DB, 1, i * 2 + (ROWS_FFN + 1))
                split_unit(dve, PH_F, i, F_G1)
                split_unit(dve, PH_F, i, F_U1)
                hidden(PH_F, i, F_U0, i * 2 + 3, 0)
                split_unit(dve, PH_F, i + 1, 0)
                split_unit(dve, PH_F, i + 1, 1)
                hidden(PH_F, i, F_U1, i * 2 + 4, 1)
            dve.wait_ge(gain_f_loaded, 16)
            for k in range(4):
                split_unit(dve, PH_F1, 0, k + 2)
                if k % 2:
                    hidden(PH_F1, 0, k, 2 * FFN_LOOPS + 3 + k // 2, k // 2, 1)
            for k in range(4, 6):
                add_rows(dve, PH_F1, 0, k, k - 4, ROWS_LAST - 2 + (k - 4))
                split_unit(dve, PH_F1, 0, k + 2)

            def scale_out(t):
                if t >= 4:
                    dve.wait_ge(out_stored[t % 4], 16)
                norm_scale(dve, 2, t, x2[:, t, :], rms3, rstd3, gain_f, out_sb[:, t % 4, :])

            for j, (u, t) in enumerate(PAIR_ORDER):
                add_pair_tile(dve, PH_F1, 6, j, ROWS_LAST)
                if u == 1 and t >= 1:
                    scale_out(t - 1)
            scale_out(TT - 1)


_INS = ["x", "norm1_g", "w_in", "w_gate_lr", "b_gate", "gla_norm_g", "w_branch_a", "w_branch_b",
        "w_out", "norm2_g", "w_ffn_in", "w_ffn_down", "norm_f_g"]
_OUTS = [((1, S, D), "float32")]


def kernel(**inputs):
    import concourse.bacc as _bacc
    from concourse.bass_utils import run_bass_kernel_spmd as _run

    nc = _bacc.Bacc("TRN2", target_bir_lowering=False, num_devices=1)
    arrays = {f"in_{name}_dram": np.ascontiguousarray(inputs[name]) for name in _INS}
    arrays["const_masks"], arrays["const_rope"] = shape_constants()
    args = [nc.dram_tensor(name, a.shape, mybir.dt.from_np(a.dtype), kind="ExternalInput").ap()
            for name, a in arrays.items()]
    for n, (shape, dtype) in enumerate(_OUTS):
        args.append(nc.dram_tensor(f"out_{n}_dram", shape, mybir.dt.from_np(np.dtype(dtype)),
                                   kind="ExternalOutput").ap())
    hybrid_block(nc, *args)
    r = _run(nc, [arrays], core_ids=[0])
    return r.results[0]["out_0_dram"]
```

```python
from contextlib import ExitStack

import numpy as np
import concourse.bass as bass
from concourse import mybir

ALU = mybir.AluOpType
ACT = mybir.ActivationFunctionType
AX = mybir.AxisListType
F32 = mybir.dt.float32
F32R = mybir.dt.float32r
I32 = mybir.dt.int32

P = 128
S = 1024
D = 1024
KC = D // P
TT = S // P
HALF = 512
HD = 128
HEADS = 4
GROUPS = 3
DIL = (1, 4, 16)
ROPE = HD // 4
ROPE_THETA = 500000.0
GV = 256
CH = 64
RANK = 16
GATE_NORM = 16.0
FFN = 2816
EPS = 1e-6
BIG = 1e30

AQ, AK, AV = 0, 1536, 3072
GQ, GK, GVC, GR, GLR, GA, GB = 4608, 5120, 5632, 6656, 7680, 7696, 8720

C_ID, C_BAND, C_PAIR, C_GLA, C_RESTART, C_END = 0, 128, 384, 512, 640, 1152


def shape_constants():
    q, k = np.arange(P)[:, None], np.arange(P)[None, :]
    blob = np.zeros((P, C_END), np.float32)
    blob[:, C_ID:C_ID + P] = q == k
    blob[:, C_BAND:C_BAND + P] = np.where(k >= q, 0.0, -BIG)
    blob[:, C_BAND + P:C_BAND + 2 * P] = np.where(k <= q, 0.0, -BIG)
    blob[:, C_PAIR:C_PAIR + P] = np.where((k <= q) & (k % 2 == q % 2), 0.0, -BIG)
    blob[:, C_GLA:C_GLA + P] = q <= k
    blob[:, C_RESTART:C_END] = (np.arange(C_END - C_RESTART) % CH != 0)[None, :]
    inv = np.float32(ROPE_THETA) ** (-np.arange(0, ROPE, 2, dtype=np.float32) / np.float32(ROPE))
    ang = np.arange(S, dtype=np.float32)[None, :] * inv.astype(np.float32)[:, None]
    ang = np.concatenate([ang, ang], axis=0)
    sign = np.where(np.arange(ROPE) < ROPE // 2, -1.0, 1.0).astype(np.float32)[:, None]
    rope = np.stack([np.cos(ang), np.sin(ang) * sign], axis=1).astype(np.float32)
    return blob, rope


class Phase:

    def __init__(self, before, iters, slots, outs):
        self.slots, self.outs, self.iters = slots, outs, iters
        self.slot_base = [before.slot_end[s] if before else 0 for s in range(2)]
        self.out_base = [before.out_end[s] if before else 0 for s in range(2)]
        self.slot_end = [b + iters * slots.count(s) for s, b in enumerate(self.slot_base)]
        self.out_end = [b + iters * outs.count(s) for s, b in enumerate(self.out_base)]

    def n(self, i, k):
        s = self.slots[k]
        return i * self.slots.count(s) + (self.slot_base[s] + self.slots[:k].count(s))

    def o(self, i, k):
        s = self.outs[k]
        return i * self.outs.count(s) + (self.out_base[s] + self.outs[:k].count(s))


PH_GLA = Phase(None, HEADS, [0, 1] * 3, [0, 1] * 3)
PH_B = Phase(PH_GLA, KC, [0, 1], [0, 1])
PH_ATT = Phase(PH_B, HEADS, [0, 1, 0, 1, 0, 1, 0, 1, 0], [0, 1, 0, 1, 0, 1, 0, 1, 0, 1])
PH_A = Phase(PH_ATT, 2, [0, 1] * 3, [0, 1, None, 0, 1, None])
PH_WO = Phase(PH_A, 1, [0, 1] * 4, [None] * 8)
PH_F0 = Phase(PH_WO, 1, [0, 1] * 2, [0, 1] * 2)
FFN_LOOPS = FFN // 256 - 2
PH_F = Phase(PH_F0, FFN_LOOPS, [0, 1] * 3, [0, None, None, 1, 0, 1])
PH_F1 = Phase(PH_F, 1, [0, 1] * 4, [0, 1, 0, 1] + [None] * 4)

PAIR_ORDER = [(0, 0), (0, 1)] + [x for t in range(TT - 2) for x in ((1, t), (0, t + 2))] + [(1, TT - 2), (1, TT - 1)]
ROWS_FFN, ROWS_LAST = 8, 8 + 2 * (FFN // 256 - 1)

G_V0, G_V1, G_K, G_Q, G_R0, G_R1 = range(6)
F_G0, F_DA, F_DB, F_U0, F_G1, F_U1 = range(6)


def score_tiles():
    out = []
    for t in range(TT):
        out.append((0, t, max(0, 2 * t - 1) * P, P if t == 0 else 2 * P))
    for r in range(4):
        out.append((1, 2 * r, 3 * r * P, P))
        out.append((1, 2 * r + 1, (3 * r + 1) * P, 2 * P))
    for t in range(TT):
        out.append((2, t, t * P, P))
    return out


def prob_blocks():
    out = []
    for g, t, off, width in score_tiles():
        first = t - (width // P - 1)
        for j in range(width // P):
            out.append((g, t, first + j, off // P + j))
    return out


def token_view(ap, g, t):
    if g == 0:
        return ap[:, t * P:(t + 1) * P]
    if g == 1:
        return ap[:, (t % 2) * HALF + t // 2:(t % 2 + 1) * HALF:4]
    return ap[:, t:S:TT]


def key_view(ap, g, t, width):
    if width == P:
        return token_view(ap, g, t)
    if g == 0:
        return ap[:, (t - 1) * P:(t + 1) * P]
    return ap[:, t // 2:S:4]


def hybrid_block(nc, x, norm1_g, w_in, w_gate_lr, b_gate, gla_norm_g, w_branch_a, w_branch_b,
                 w_out, norm2_g, w_ffn_in, w_ffn_down, norm_f_g, blob, rope, out):
    x_tiles = x[0].rearrange("(t p) d -> t p d", p=P)
    out_tiles = out[0].rearrange("(t p) d -> t p d", p=P)
    win = w_in[0].rearrange("(k p) n -> p k n", p=P)
    wa = w_branch_a[0].rearrange("(k p) n -> p k n", p=P)
    wb = w_branch_b[0].rearrange("(k p) n -> p k n", p=P)
    wo = w_out[0].rearrange("(k p) n -> p k n", p=P)
    wfi = w_ffn_in[0].rearrange("(k p) n -> p k n", p=P)
    wfd = w_ffn_down[0].rearrange("(k p) n -> p k n", p=P)
    stats_dram = nc.dram_tensor("stats_dram", (S, 2 * GROUPS), F32, kind="Internal").ap()

    with ExitStack() as ctx:
        ctx.enter_context(nc.allow_non_contiguous_dma(reason="a few thousand single values"))
        base = -(-nc.sbuf_base // 64) * 64

        def sb(name, at_kb, shape, dtype=F32):
            return nc.alloc_sbuf_tensor_at(name, shape, dtype, offset=base + int(at_kb * 1024))

        def sem(name):
            return ctx.enter_context(nc.semaphore(name))

        ht_hi = sb("ht_hi", 0, [P, KC, S], F32R)
        ht_lo = sb("ht_lo", 32, [P, KC, S], F32R)
        raw = [sb(f"raw{s}", 64 + 4 * s, [P, S]) for s in range(2)]
        whi = [sb(f"whi{s}", 72 + 8 * s, [P, S], F32R) for s in range(2)]
        wlo = [sb(f"wlo{s}", 76 + 8 * s, [P, S], F32R) for s in range(2)]
        consts = sb("consts", 88, [P, C_END])
        small = sb("small", 92.75, [P, 288])
        rope_sb = sb("rope_sb", 94, [ROPE, 2, S])
        x_in = sb("x_in", 102, [P, TT, D])
        gain1 = sb("gain1", 134, [P, D])
        square1 = sb("square1", 138, [P, D])
        xn = sb("xn", 142, [P, 4, D])
        glr_raw = sb("glr_raw", 158, [P, KC, RANK])
        glr_weights = sb("glr_weights", 159, [P, KC, 4, 2, RANK], F32R)
        v_tok = sb("v_tok", 102, [P, TT, GV])
        k_end = sb("k_end", 110, [P, S])
        o_tok = sb("o_tok", 110, [P, TT, GV])
        k_dec = sb("k_dec", 118, [P, S])
        q_dec = sb("q_dec", 122, [P, S])
        q_int = sb("q_int", 126, [P, S])
        k_tok = sb("k_tok", 130, [P, TT, P])
        gla_raw = sb("gla_raw", 134, [P, KC, S])
        att_t = sb("att_t", 166, [P, TT, P])
        gla_silu = sb("gla_silu", 170, [P, 2, S])
        b_cum = sb("b_cum", 178, [P, S])
        diff1 = sb("diff1", 182, [P, S])
        diff2 = sb("diff2", 186, [P, S])
        exp_a = sb("exp_a", 190, [P, S])
        exp_b = sb("exp_b", 194, [P, S])
        glr_t = sb("glr_t", 198, [P, S], F32R)
        state = sb("state", 202, [P, 4, GV])
        square_g = sb("square_g", 206, [P, GV])
        k_cross = sb("k_cross", 94, [P, TT, CH])
        q_cross = sb("q_cross", 96, [P, TT, CH])
        mix = sb("mix", 102, [P, KC, S])
        gla_lo = sb("gla_lo", 134, [P, KC, S], F32R)
        gla_hi = sb("gla_hi", 166, [P, KC, S], F32R)
        gate_b = sb("gate_b", 198, [P, S])
        attn_raw = sb("attn_raw", 134, [P, HEADS, S])
        qkv = [sb(f"qkv{r}", 150 + 4 * r, [P, S]) for r in range(3)]
        prob = [sb("prob0", 162, [P, 15 * P]), sb("prob1", 169.5, [P, 12 * P]),
                sb("prob2", 175.5, [P, 8 * P])]
        va_tok = sb("va_tok", 179.5, [P, GROUPS, TT, HD])
        prob_t = sb("prob_t", 191.5, [P, 3, HALF])
        rotated = sb("rotated", 197.5, [ROPE, S])
        own_stats = sb("own_stats", 202, [P, GROUPS, TT, 2])
        neg_max = sb("neg_max", 202.25, [P, GROUPS, TT])
        all_stats = sb("all_stats", 202.5, [P, GROUPS, TT, 2 * GROUPS])
        top = sb("top", 203.25, [P, GROUPS * TT])
        shifted = sb("shifted", 203.5, [P, GROUPS * TT, GROUPS])
        scaled = sb("scaled", 204, [P, GROUPS * TT, GROUPS])
        total = sb("total", 204.5, [P, GROUPS * TT])
        weight = sb("weight", 204.75, [P, GROUPS, TT])
        attn_hi = sb("attn_hi", 166, [P, HEADS, S], F32R)
        attn_lo = sb("attn_lo", 182, [P, HEADS, S], F32R)
        gate_a = sb("gate_a", 198, [P, 2, S])
        mix_lo = sb("mix_lo", 102, [P, KC, S], F32R)
        mix_hi = sb("mix_hi", 134, [P, KC, S], F32R)
        x2 = sb("x2", 0, [P, TT, D])
        h2_lo = sb("h2_lo", 32, [P, KC, S], F32R)
        h2_hi = sb("h2_hi", 166, [P, KC, S], F32R)
        gain2 = sb("gain2", 94, [P, D])
        gain_f = sb("gain_f", 98, [P, D])
        xn2 = sb("xn2", 102, [P, 4, D])
        out_sb = sb("out_sb", 102, [P, 4, D])
        square2 = sb("square2", 118, [P, D])
        silu_g = sb("silu_g", 122, [P, S])
        gated = sb("gated", 126, [P, S])
        act_hi = [sb(f"act_hi{n}", 134 + 16 * n, [P, 2, S], F32R) for n in range(2)]
        act_lo = [sb(f"act_lo{n}", 142 + 16 * n, [P, 2, S], F32R) for n in range(2)]

        ident = consts[:, C_ID:C_ID + P]
        band = consts[:, C_BAND:C_BAND + 2 * P]
        pair = consts[:, C_PAIR:C_PAIR + P]
        gla_mask = consts[:, C_GLA:C_GLA + P]
        restart = consts[:, C_RESTART:C_END]
        eps = small[:, 0:1]
        one = small[:, 1:2]
        ss1, rms1, rstd1 = small[:, 8:16], small[:, 16:24], small[:, 24:32]
        ss2, rms2, rstd2 = small[:, 32:40], small[:, 40:48], small[:, 48:56]
        ss3, rms3, rstd3 = small[:, 56:64], small[:, 64:72], small[:, 72:80]
        ssg, rmsg, rstdg = small[:, 80:88], small[:, 88:96], small[:, 96:104]
        b_gate_sb = small[:, 104:108]
        gla_gain = small[:, 108:110]
        b_gate_head = small[:, 110:111]
        decay = small[:, 112:128]
        decay_two = small[:, 128:136]
        w_gate_head = sb("w_gate_head", 98, [P, P])
        w_gate_parts = sb("w_gate_parts", 98.5, [P, P], F32R)

        proj = [ctx.enter_context(nc.psum_tensor(f"proj{b}", [P, S], F32)) for b in range(2)]
        aux = ctx.enter_context(nc.psum_tensor("aux", [P, 4, HALF], F32))
        aux_a = aux[:, 0:2, :].rearrange("p a b -> p (a b)")
        aux_b = aux[:, 2:4, :].rearrange("p a b -> p (a b)")

        glr_raw_four = glr_raw[:, :, :].rearrange("p k (a r) -> p k a r", a=1).to_broadcast([P, KC, 4, RANK])

        def output_psum(t):
            return aux[:, t % 2, 0:GV]

        loaded = [sem(f"loaded{s}") for s in range(2)]
        rounded = [sem(f"rounded{s}") for s in range(2)]
        split = [sem(f"split{s}") for s in range(2)]
        multiplied = [sem(f"multiplied{s}") for s in range(2)]
        out_read = [sem(f"out_read{s}") for s in range(2)]

        passed = {e.engine: sem(f"passed_{n}") for n, e in
                  (("sync", nc.sync), ("vector", nc.vector), ("gpsimd", nc.gpsimd))}
        ident_loaded = sem("ident_loaded")
        masks_loaded = sem("masks_loaded")
        gain1_loaded = sem("gain1_loaded")
        gla_gain_loaded = sem("gla_gain_loaded")
        const_set = sem("const_set")
        rope_loaded = sem("rope_loaded")
        x_loaded = [sem(f"x_loaded{t}") for t in range(TT)]
        x2_loaded = [sem(f"x2_loaded{t}") for t in range(TT)]
        gains_loaded = sem("gains_loaded")
        gain_f_loaded = sem("gain_f_loaded")
        norm_sem = [{k: sem(f"norm{n}_{k}") for k in
                     ("squared", "root", "recip", "scaled", "turned", "hi", "lo")} for n in (1, 2, 3)]

        glr_loaded = sem("glr_loaded")
        glr_rounded = sem("glr_rounded")
        glr_split = sem("glr_split")
        glr_done = sem("glr_done")
        glr_hi_ready = sem("glr_hi_ready")
        glr_ready = sem("glr_ready")
        gate_weights_loaded = sem("gate_weights_loaded")
        gate_weights_rounded = sem("gate_weights_rounded")
        gate_weights_split = sem("gate_weights_split")
        z_done = sem("z_done")
        soft_step = sem("soft_step")
        soft_ready = sem("soft_ready")
        z_clamped = sem("z_clamped")
        log_a_ready = sem("log_a_ready")
        cumsum_done = sem("cumsum_done")
        diffs_ready = sem("diffs_ready")
        k_exps_ready = sem("k_exps_ready")
        q_exps_ready = sem("q_exps_ready")
        k_scaled = sem("k_scaled")
        k_read = sem("k_read")
        q_read = sem("q_read")
        cross_ready = sem("cross_ready")
        q_scaled = sem("q_scaled")
        v_half_done = sem("v_half_done")
        v_read = sem("v_read")
        gla_turned = sem("gla_turned")
        gla_turn_read = sem("gla_turn_read")
        att_t_cleared = sem("att_t_cleared")
        att_t_done = sem("att_t_done")
        att_t_ready = sem("att_t_ready")
        update_done = sem("update_done")
        state_ready = sem("state_ready")
        o_done = sem("o_done")
        o_read = sem("o_read")
        gla_squared = sem("gla_squared")
        gla_root = sem("gla_root")
        gla_recip = sem("gla_recip")
        o_normed = sem("o_normed")
        o_turned = sem("o_turned")
        gate_r_ready = sem("gate_r_ready")
        gla_written = sem("gla_written")
        gla_hi_ready = sem("gla_hi_ready")
        gla_lo_ready = sem("gla_lo_ready")

        qk_copied = sem("qk_copied")
        rope_step = sem("rope_step")
        qk_ready = sem("qk_ready")
        va_ready = sem("va_ready")
        va_turned = sem("va_turned")
        va_tok_ready = sem("va_tok_ready")
        scores_done = sem("scores_done")
        scores_masked = sem("scores_masked")
        neg_max_ready = sem("neg_max_ready")
        exps_done = sem("exps_done")
        stats_stored = [sem(f"stats_stored{g}") for g in range(GROUPS)]
        stats_back = [sem(f"stats_back{g}") for g in range(GROUPS)]
        combine_step = sem("combine_step")
        shift_exp_ready = sem("shift_exp_ready")
        weight_ready = sem("weight_ready")
        prob_weighted = sem("prob_weighted")
        prob_turned = sem("prob_turned")
        prob_t_ready = sem("prob_t_ready")
        pv_done = sem("pv_done")
        attn_written = sem("attn_written")
        attn_hi_ready = sem("attn_hi_ready")
        attn_lo_ready = sem("attn_lo_ready")

        branch_a_half = sem("branch_a_half")
        gate_a_step = sem("gate_a_step")
        gated_a = sem("gated_a")
        mix_hi_ready = sem("mix_hi_ready")
        mix_lo_ready = sem("mix_lo_ready")
        rows_done = sem("rows_done")
        rows_added = sem("rows_added")
        gated_ready = sem("gated_ready")
        act_hi_ready = sem("act_hi_ready")
        act_lo_ready = sem("act_lo_ready")
        out_stored = [sem(f"out_stored{b}") for b in range(4)]

        block = ctx.enter_context(nc.Block())

        def wait_apart(eng, semaphore, value):
            eng.wait_ge(semaphore, value)
            eng.sem_inc(passed[eng.engine], 1)

        def load_unit(sp, ph, i, k, dst, src):
            s = ph.slots[k]
            wait_apart(sp, split[s], ph.n(i, k) + 1)
            sp.dma_start(dst, src).then_inc(loaded[s], 16)

        def round_unit(act, ph, i, k, cols=S):
            s = ph.slots[k]
            act.wait_ge(loaded[s], (ph.n(i, k) + 1) * 16)
            act.wait_ge(multiplied[s], ph.n(i, k) + 1)
            act.activation(whi[s][:, 0:cols], raw[s][:, 0:cols], ACT.Copy).then_inc(rounded[s], 1)

        def split_unit(dve, ph, i, k, cols=S):
            s = ph.slots[k]
            dve.wait_ge(rounded[s], ph.n(i, k) + 1)
            dve.tensor_tensor(wlo[s][:, 0:cols], raw[s][:, 0:cols], whi[s][:, 0:cols].bitcast(F32),
                              ALU.subtract).then_inc(split[s], 1)

        def slot_weights(s, k_chunks, cols):
            n = k_chunks * cols
            return (whi[s][:, 0:n].rearrange("p (k n) -> p k n", k=k_chunks),
                    wlo[s][:, 0:n].rearrange("p (k n) -> p k n", k=k_chunks))

        def three_products(pe, dst, chunks, chunk_ready=None):
            last = 3 * len(chunks) - 1
            for c, (a_hi, a_lo, b_hi, b_lo) in enumerate(chunks):
                if chunk_ready is not None:
                    pe.wait_ge(chunk_ready, c + 1)
                pe.matmul(dst, a_hi, b_lo, start=(c == 0), stop=False)
                pe.matmul(dst, a_lo, b_hi, start=False, stop=False)
                mm = pe.matmul(dst, a_hi, b_hi, start=False, stop=(3 * c + 2 == last))
            return mm

        def feature_half(pe, ph, i, k, hi, lo, h, rows_ready=None):
            s, o = ph.slots[k], ph.outs[k]
            w_h, w_l = slot_weights(s, KC, P)
            if h == 0:
                pe.wait_ge(split[s], ph.n(i, k) + 2)
                pe.wait_ge(out_read[o], ph.o(i, k) + 1)
            cols = slice(h * HALF, (h + 1) * HALF)
            mm = three_products(pe, proj[o][:, cols],
                                [(w_h[:, c, :], w_l[:, c, :], hi[:, c, cols], lo[:, c, cols])
                                 for c in range(KC)], rows_ready if h == 0 else None)
            if h == 1:
                mm.then_inc(multiplied[s], 1)

        def feature_unit(pe, ph, i, k, hi, lo, rows_ready=None):
            for h in range(2):
                feature_half(pe, ph, i, k, hi, lo, h, rows_ready)

        def low_rank_half(pe, h):
            cols = slice(h * HALF, (h + 1) * HALF)
            for c in range(KC):
                for part in (ht_lo, ht_hi):
                    mm = pe.matmul(aux_a[:, cols], glr_weights[:, c, :, :, :].rearrange("p a b r -> p (a b r)"), part[:, c, cols],
                                   start=(c == 0 and part is ht_lo), stop=(c == KC - 1 and part is ht_hi))
            return mm

        def unit_multiplied(eng, ph, i, k):
            eng.wait_ge(multiplied[ph.slots[k]], ph.n(i, k) + 2)

        def row_unit(pe, ph, i, k, hi, lo, row):
            for t in range(TT):
                if ph is PH_WO and k == 0 and t % 2 == 0 and t < 4:
                    pe.wait_ge(gate_a_step, KC + 1 + t // 2)
                row_tile(pe, ph, i, k, hi, lo, t, t, row)

        def row_tile(pe, ph, i, k, hi, lo, t, j, row):
            s = ph.slots[k]
            w_h, w_l = slot_weights(s, 2, HALF)
            if t == 0:
                pe.wait_ge(split[s], ph.n(i, k) + 2)
            pe.wait_ge(rows_added, row * TT + (j + 1))
            cols = slice(t * P, (t + 1) * P)
            mm = three_products(pe, aux[:, j % 4, :],
                                [(hi[:, c, cols], lo[:, c, cols], w_h[:, c, :], w_l[:, c, :])
                                 for c in range(2)])
            mm.then_inc(*((rows_done, 1) if t < TT - 1 else (multiplied[s], 1)))

        def add_rows(dve, ph, i, k, half, row):
            for t in range(TT):
                if ph is PH_WO and k < 2:
                    dve.wait_ge(x2_loaded[t], 16)
                if t < TT - 1:
                    dve.wait_ge(rows_done, row * (TT - 1) + (t + 1))
                else:
                    unit_multiplied(dve, ph, i, k)
                dst = x2[:, t, half * HALF:(half + 1) * HALF]
                dve.tensor_tensor(dst, aux[:, t % 4, :], dst, ALU.add).then_inc(rows_added, 1)

        def add_pair_tile(dve, ph, first, j, row):
            u, t = PAIR_ORDER[j]
            if t < TT - 1:
                signalled = sum(tile < TT - 1 for _, tile in PAIR_ORDER[:j + 1])
                dve.wait_ge(rows_done, row * (TT - 1) + signalled)
            else:
                unit_multiplied(dve, ph, 0, first + u)
            dst = x2[:, t, u * HALF:(u + 1) * HALF]
            dve.tensor_tensor(dst, aux[:, j % 4, :], dst, ALU.add).then_inc(rows_added, 1)

        def pair_added(eng, t, row):
            eng.wait_ge(rows_added, 4 + row * TT + PAIR_ORDER.index((1, t)) + 1)

        def norm_root(act, n, t, src, square, ss, rms):
            sems = norm_sem[n]
            act.activation(square[:, :], src, ACT.Square, accum_out=ss[:, t:t + 1])\
               .then_inc(sems["squared"], 1)
            act.wait_ge(sems["squared"], t + 1)
            act.activation(rms[:, t:t + 1], ss[:, t:t + 1], ACT.Sqrt, bias=eps, scale=1.0 / D)\
               .then_inc(sems["root"], 1)

        def norm_scale(dve, n, t, src, rms, rstd, gain, dst):
            sems = norm_sem[n]
            dve.wait_ge(sems["root"], t + 1)
            dve.reciprocal(rstd[:, t:t + 1], rms[:, t:t + 1]).then_inc(sems["recip"], 1)
            dve.wait_ge(sems["recip"], t + 1)
            dve.scalar_tensor_tensor(dst, src, rstd[:, t:t + 1], gain[:, :], ALU.mult, ALU.mult)\
               .then_inc(sems["scaled"], 1)

        def turn_psum(n, t):
            if n == 1:
                return proj[(t + 1) % 2][:, :] if t < 5 else (aux_b, aux_a)[t % 2]
            return (aux_a, aux_b)[t % 2]

        def norm_turn(pe, n, t, src):
            sems = norm_sem[n]
            pe.wait_ge(sems["scaled"], t + 1)
            if n == 1 and t in (5, 6):
                pe.wait_ge(rows_added, 4 + ROWS_FFN * TT - (2 if t == 5 else 0))
            elif t >= 2:
                pe.wait_ge(sems["lo"], t - 1)
            for c in range(KC):
                mm = pe.transpose(turn_psum(n, t)[:, c * P:(c + 1) * P], src[:, c * P:(c + 1) * P], ident)
            mm.then_inc(sems["turned"], 1)

        def norm_hi(act, n, t, hi):
            act.wait_ge(norm_sem[n]["turned"], t + 1)
            act.activation(hi[:, :, t * P:(t + 1) * P], turn_psum(n, t).rearrange("p (c q) -> p c q", c=KC),
                           ACT.Copy).then_inc(norm_sem[n]["hi"], 1)

        def norm_lo(dve, n, t, hi, lo):
            cols = slice(t * P, (t + 1) * P)
            dve.wait_ge(norm_sem[n]["hi"], t + 1)
            dve.tensor_tensor(lo[:, :, cols], turn_psum(n, t).rearrange("p (c q) -> p c q", c=KC),
                              hi[:, :, cols].bitcast(F32), ALU.subtract).then_inc(norm_sem[n]["lo"], 1)

        def feature_raw(s, k_chunks=KC, cols=P):
            return raw[s][:, 0:k_chunks * cols].rearrange("p (k n) -> p k n", k=k_chunks)

        @block.sync
        def _(sp):
            def load_value_weights(i, k):
                load_unit(sp, PH_GLA, i, k, feature_raw(k % 2, 4, GV),
                          win[:, 4 * (k % 2):4 * (k % 2) + 4, bass.ds(i * GV + GVC, GV)])

            def load_gate_weights(i):
                sp.dma_start(w_gate_head[:, :], w_gate_lr[0][:, bass.ds(i * P, P)]
                             .rearrange("(a r) n -> a r n", a=1).to_broadcast([P // RANK, RANK, P]))\
                  .then_inc(gate_weights_loaded, 16)
                sp.dma_start(b_gate_head, b_gate[0][bass.ds(i * P, P)].rearrange("(p a) -> p a", a=1))\
                  .then_inc(gate_weights_loaded, 16)

            for t in range(TT):
                sp.dma_start(x_in[:, t, :], x_tiles[t]).then_inc(x_loaded[t], 16)
                if t == 0:
                    sp.dma_start(gain1[:, :], norm1_g.to_broadcast([P, D])).then_inc(gain1_loaded, 16)
                if t in (1, 2):
                    load_value_weights(0, (G_V0, G_V1)[t - 1])
            sp.dma_start(glr_raw[:, :, :], win[:, :, GLR:GLR + RANK]).then_inc(glr_loaded, 16)
            load_gate_weights(0)

            def gla_loads(i, first):
                if not first:
                    load_value_weights(i, G_V0)
                    load_gate_weights(i)
                    load_value_weights(i, G_V1)
                for k, col in ((G_K, i * P + GK), (G_Q, i * P + GQ),
                               (G_R0, i * GV + GR), (G_R1, i * GV + (GR + P))):
                    load_unit(sp, PH_GLA, i, k, feature_raw(k % 2), win[:, :, bass.ds(col, P)])

            gla_loads(0, True)
            with sp.Fori(1, HEADS) as i:
                gla_loads(i, False)
            with sp.Fori(0, KC) as i:
                load_unit(sp, PH_B, i, 0, feature_raw(0), win[:, :, bass.ds(i * P + GB, P)])
                load_unit(sp, PH_B, i, 1, feature_raw(1), wb[:, :, bass.ds(i * P, P)])
            with sp.Fori(0, HEADS) as i:
                for k in range(9):
                    g, col = (k // 2, (AQ, AK)[k % 2]) if k < 6 else (k - 6, AV)
                    load_unit(sp, PH_ATT, i, k, feature_raw(k % 2),
                              win[:, :, bass.ds(i * P + (col + g * HEADS * P), P)])
            with sp.Fori(0, 2) as i:
                for m in range(2):
                    for b in range(2):
                        load_unit(sp, PH_A, i, 3 * m + b, feature_raw((3 * m + b) % 2),
                                  win[:, :, bass.ds(i * HALF + (GA + (2 * m + b) * P), P)])
                    load_unit(sp, PH_A, i, 3 * m + 2, feature_raw((3 * m + 2) % 2, 4, 2 * P),
                              wa[:, :, bass.ds(i * HALF + 2 * m * P, 2 * P)])
            def load_w_out(k):
                load_unit(sp, PH_WO, 0, k, feature_raw(k % 2, 2, HALF),
                          wo[:, k // 2 * 2:k // 2 * 2 + 2, k % 2 * HALF:(k % 2 + 1) * HALF])

            load_w_out(0)
            load_w_out(1)
            sp.wait_ge(multiplied[PH_A.slots[4]], PH_A.n(1, 4) + 2)
            for t in range(TT):
                sp.dma_start(x2[:, t, :], x_tiles[t]).then_inc(x2_loaded[t], 16)
            for k in range(2, 8):
                load_w_out(k)

            def ffn_in(ph, i, k, part, b, up):
                load_unit(sp, ph, i, k, feature_raw(ph.slots[k]),
                          wfi[:, :, bass.ds(part * 256 + (b * P + up * FFN), P)])

            def ffn_down(ph, i, k, part, half):
                load_unit(sp, ph, i, k, feature_raw(ph.slots[k], 2, HALF),
                          wfd[:, bass.ds(part * 2, 2), half * HALF:(half + 1) * HALF])

            for k in range(4):
                ffn_in(PH_F0, 0, k, 0, k // 2, k % 2)
            with sp.Fori(0, FFN_LOOPS) as i:
                ffn_in(PH_F, i, F_G0, i + 1, 0, 0)
                ffn_down(PH_F, i, F_DA, i, 0)
                ffn_down(PH_F, i, F_DB, i, 1)
                ffn_in(PH_F, i, F_U0, i + 1, 0, 1)
                ffn_in(PH_F, i, F_G1, i + 1, 1, 0)
                ffn_in(PH_F, i, F_U1, i + 1, 1, 1)
            for k in range(4):
                ffn_in(PH_F1, 0, k, FFN_LOOPS + 1, k // 2, k % 2)
            for k in range(4, 8):
                ffn_down(PH_F1, 0, k, FFN_LOOPS + (k - 4) // 2, k % 2)
            for t in range(TT):
                sp.wait_ge(norm_sem[2]["scaled"], t + 1)
                sp.dma_start(out_tiles[t], out_sb[:, t % 4, :]).then_inc(out_stored[t % 4], 16)
            for b in range(4):
                sp.wait_ge(out_stored[b], 32)

        @block.gpsimd
        def _(pool):
            pool.memset(eps, EPS).then_inc(const_set, 1)
            pool.memset(one, 1.0).then_inc(const_set, 1)
            pool.dma_start(ident, blob[:, C_ID:C_ID + P]).then_inc(ident_loaded, 16)
            pool.wait_ge(x_loaded[TT - 1], 16)
            pool.dma_start(consts[:, C_BAND:C_END], blob[:, C_BAND:C_END]).then_inc(masks_loaded, 16)
            pool.dma_start(gla_gain, gla_norm_g[0].rearrange("(a p) -> p a", p=P)).then_inc(gla_gain_loaded, 16)

            natural = stats_dram.rearrange("(t p) s -> p t s", p=P)
            by4 = stats_dram.rearrange("(n p r) s -> p r n s", r=4, n=2)
            by16 = stats_dram.rearrange("(p t) s -> p t s", t=TT)
            pool.wait_ge(gla_lo_ready, KC)
            pool.dma_start(rope_sb[:, :, :], rope).then_inc(rope_loaded, 16)
            with pool.Fori(0, HEADS) as i:
                for g in range(GROUPS):
                    cols = slice(2 * g, 2 * g + 2)
                    wait_apart(pool, exps_done, i * (GROUPS * TT) + (g + 1) * TT)
                    if g == 0:
                        pool.dma_start(natural[:, :, cols], own_stats[:, 0, :, :]).then_inc(stats_stored[0], 16)
                    elif g == 1:
                        for r in range(4):
                            pool.dma_start(by4[:, r, :, cols], own_stats[:, 1, 2 * r:2 * r + 2, :])\
                                .then_inc(stats_stored[1], 16)
                    else:
                        pool.dma_start(by16[:, :, cols], own_stats[:, 2, :, :]).then_inc(stats_stored[2], 16)
                pool.wait_ge(stats_stored[0], i * 16 + 16)
                pool.wait_ge(stats_stored[1], i * 64 + 64)
                wait_apart(pool, stats_stored[2], i * 16 + 16)
                pool.dma_start(all_stats[:, 0, :, :], natural).then_inc(stats_back[0], 16)
                for r in range(4):
                    pool.dma_start(all_stats[:, 1, 2 * r:2 * r + 2, :], by4[:, r, :, :]).then_inc(stats_back[1], 16)
                pool.dma_start(all_stats[:, 2, :, :], by16).then_inc(stats_back[2], 16)
                pool.wait_ge(stats_back[0], i * 16 + 16)
                pool.wait_ge(stats_back[1], i * 64 + 64)
                pool.wait_ge(stats_back[2], i * 16 + 16)
            pool.dma_start(gain2[:, :], norm2_g.to_broadcast([P, D])).then_inc(gains_loaded, 16)
            pool.dma_start(gain_f[:, :], norm_f_g.rearrange("(a n) -> a n", a=1).to_broadcast([P, D]))\
                .then_inc(gain_f_loaded, 16)

        @block.tensor
        def _(pe):
            for s in range(2):
                pe.sem_inc(multiplied[s], 1)
            pe.wait_ge(ident_loaded, 16)
            def value_tile(i, k, t):
                s = PH_GLA.slots[k]
                w_h, w_l = slot_weights(s, 4, GV)
                if t == 0:
                    pe.wait_ge(split[s], PH_GLA.n(i, k) + 2)
                if k == G_V0 and t % 4 == 0:
                    pe.wait_ge(out_read[t // 4], PH_GLA.o(i, t // 4) + 1)
                cols = slice(t * P, (t + 1) * P)
                dst = proj[t // 4][:, t % 4 * GV:(t % 4 + 1) * GV]
                for c in range(4):
                    a_hi, a_lo = ht_hi[:, 4 * k + c, cols], ht_lo[:, 4 * k + c, cols]
                    for n, (a, b) in enumerate(((a_hi, w_l), (a_lo, w_h), (a_hi, w_h))):
                        mm = pe.matmul(dst, a, b[:, c, :], start=(k + c + n + t % 2 == 0),
                                       stop=(k == G_V1 and c == 3 and n == 2), skip_group_check=True)
                if t == TT - 1:
                    mm.then_inc(multiplied[s], 1)
                elif k == G_V1 and t == 3:
                    mm.then_inc(v_half_done, 1)

            for t in range(TT + 1):
                if t < TT:
                    norm_turn(pe, 0, t, xn[:, t % 4, :])
                if t >= 1:
                    pe.wait_ge(norm_sem[0]["lo"], t)
                    if t == TT:
                        pe.wait_ge(glr_split, 1)
                        for h in range(2):
                            mm = low_rank_half(pe, h)
                        mm.then_inc(glr_done, 1)
                    for k in (G_V0, G_V1):
                        value_tile(0, k, t - 1)

            def gla_head(i, first):
                def gate_logits():
                    pe.wait_ge(gate_weights_split, i * 2 + 2)
                    pe.wait_ge(glr_ready, 1)
                    pe.wait_ge(gla_written, i * 2 + 1)
                    for h in range(2):
                        mm = pe.matmul(aux_a[:, h * HALF:(h + 1) * HALF], w_gate_parts[:, :],
                                       glr_t[:, h * HALF:(h + 1) * HALF], start=True, stop=True)
                    mm.then_inc(z_done, 1)

                if not first:
                    for t in range(TT):
                        value_tile(i, G_V0, t)
                    gate_logits()
                    for t in range(TT):
                        value_tile(i, G_V1, t)
                else:
                    gate_logits()
                feature_unit(pe, PH_GLA, i, G_K, ht_hi, ht_lo)
                feature_unit(pe, PH_GLA, i, G_Q, ht_hi, ht_lo)
                pe.wait_ge(k_scaled, i + 1)
                for t in range(TT):
                    mm = pe.transpose(aux_b[:, t * P:(t + 1) * P], k_end[:, t * P:(t + 1) * P], ident)
                mm.then_inc(gla_turned, 1)
                feature_unit(pe, PH_GLA, i, G_R0, ht_hi, ht_lo)
                pe.wait_ge(att_t_cleared, 1)
                pe.wait_ge(q_scaled, i + 1)
                for t in range(TT):
                    cols = slice(t * P, (t + 1) * P)
                    pe.matmul(aux_a[:, cols], k_dec[:, cols], q_dec[:, cols], start=True, stop=True)
                    mm = pe.matmul(aux_a[0:CH, t * P + CH:(t + 1) * P], k_cross[:, t, :], q_cross[:, t, :],
                                   start=True, stop=True)
                mm.then_inc(att_t_done, 1)
                pe.wait_ge(v_read, i * 2 + 2)
                pe.wait_ge(gla_turn_read, i + 1)

                def update(t):
                    if t >= 2:
                        pe.wait_ge(state_ready, i * 7 + (t - 1))
                    pe.matmul(aux[:, 2 + t % 2, 0:GV], k_tok[:, t, :], v_tok[:, t, :],
                              start=True, stop=True).then_inc(update_done, 1)

                update(0)
                update(1)
                for t in range(TT):
                    if t < 2:
                        pe.wait_ge(att_t_ready, i * 2 + (t + 1))
                    if t >= 2:
                        pe.wait_ge(o_read, i * TT + (t - 1))
                    mm = pe.matmul(output_psum(t), att_t[:, t, :], v_tok[:, t, :], start=True, stop=(t == 0))
                    if t:
                        pe.wait_ge(state_ready, i * 7 + t)
                        mm = pe.matmul(output_psum(t), q_int[:, t * P:(t + 1) * P], state[:, t % 4, :],
                                       start=False, stop=True)
                    mm.then_inc(o_done, 1)
                    if t + 2 < TT - 1:
                        update(t + 2)
                feature_unit(pe, PH_GLA, i, G_R1, ht_hi, ht_lo)
                pe.wait_ge(o_normed, i + 1)
                for v, dst in enumerate((aux_a, aux_b)):
                    for t in range(TT):
                        mm = pe.transpose(dst[:, t * P:(t + 1) * P], o_tok[:, t, v * P:(v + 1) * P], ident)
                    mm.then_inc(o_turned, 1)

            gla_head(0, True)
            with pe.Fori(1, HEADS) as i:
                gla_head(i, False)

            with pe.Fori(0, KC) as i:
                feature_unit(pe, PH_B, i, 0, ht_hi, ht_lo)
                feature_unit(pe, PH_B, i, 1, gla_hi, gla_lo, gla_lo_ready)

            with pe.Fori(0, HEADS) as i:
                def scores(g):
                    pe.wait_ge(qk_ready, i * 6 + (2 * g + 2))
                    q, k = qkv[2 * g % 3], qkv[(2 * g + 1) % 3]
                    tiles = [x for x in score_tiles() if x[0] == g]
                    for n, (_, t, off, width) in enumerate(tiles):
                        if g == 0 and n == 0:
                            pe.wait_ge(prob_t_ready, i * 9 + 1)
                            pe.wait_ge(attn_written, i * 2 + 1)
                        elif g > 0 and n == 0:
                            pe.wait_ge(scores_masked, i * 24 + 8 * g)
                        pe.matmul(aux[:, n // 2, n % 2 * 2 * P:n % 2 * 2 * P + width],
                                  token_view(q, g, t), key_view(k, g, t, width),
                                  start=True, stop=True).then_inc(scores_done, 1)

                def turn_values(g, bank):
                    pe.wait_ge(va_ready, i * 3 + (g + 1))
                    for t in range(TT):
                        mm = pe.transpose(aux[:, bank + t // 4, t % 4 * P:(t % 4 + 1) * P],
                                          token_view(qkv[g], g, t), ident)
                    mm.then_inc(va_turned, 1)

                for k in range(9):
                    feature_half(pe, PH_ATT, i, k, ht_hi, ht_lo, 0)
                    if k == 8:
                        turn_values(1, 2)
                    feature_half(pe, PH_ATT, i, k, ht_hi, ht_lo, 1)
                    if k in (2, 4, 6):
                        scores(k // 2 - 1)
                    if k == 7:
                        pe.wait_ge(scores_masked, i * 24 + 24)
                        turn_values(0, 0)
                blocks = prob_blocks()
                chunks = [blocks[c:c + 4] for c in range(0, len(blocks), 4)]
                started = set()

                def turn_probs(c):
                    if c < 2:
                        pe.wait_ge(va_tok_ready, i * 3 + 2)
                    else:
                        pe.wait_ge(prob_t_ready, i * 9 + (c - 1 + 1))
                    g, t = chunks[c][-1][:2]
                    pe.wait_ge(prob_weighted, i * 24 + (8 * g + t + 1))
                    for j, (g, t, kt, col) in enumerate(chunks[c]):
                        mm = pe.transpose(aux[:, 2 + c % 2, j * P:(j + 1) * P],
                                          prob[g][:, col * P:(col + 1) * P], ident)
                    mm.then_inc(prob_turned, 1)

                def values(c):
                    pe.wait_ge(prob_t_ready, i * 9 + (c + 1 + 1))
                    if c == 0:
                        pe.wait_ge(out_read[1], PH_ATT.o(i, 9) + 1)
                    for j, (g, t, kt, col) in enumerate(chunks[c]):
                        src = prob_t[:, c % 3, j * P:(j + 1) * P]
                        if g == 2:
                            if t == 0:
                                pe.wait_ge(va_tok_ready, i * 3 + 3)
                            mm = pe.matmul(aux_a[:, t * P:(t + 1) * P], va_tok[:, g, kt, :], src,
                                           start=True, stop=True)
                        else:
                            bank = t // 4 if g == 0 else t % 2
                            mm = pe.matmul(token_view(proj[1], g, t), va_tok[:, g, kt, :], src,
                                           start=bank not in started, stop=True, skip_group_check=True)
                            started.add(bank)
                    return mm

                for c in range(len(chunks) + 2):
                    if c < len(chunks):
                        turn_probs(c)
                    if c == 1:
                        pe.wait_ge(va_tok_ready, i * 3 + 1)
                        turn_values(2, 0)
                    if c >= 2:
                        mm = values(c - 2)
                mm.then_inc(pv_done, 1)

            with pe.Fori(0, 2) as i:
                for m in range(2):
                    for b in range(2):
                        feature_unit(pe, PH_A, i, 3 * m + b, ht_hi, ht_lo)
                    k = 3 * m + 2
                    w_h, w_l = slot_weights(PH_A.slots[k], 4, 2 * P)
                    pe.wait_ge(split[PH_A.slots[k]], PH_A.n(i, k) + 2)
                    pe.wait_ge(attn_lo_ready, HEADS)
                    for b in range(2):
                        pe.wait_ge(gate_a_step, i * 4 + (2 * m + b + 1))
                        for h in range(2):
                            cols = slice(h * HALF, (h + 1) * HALF)
                            feats = slice(b * P, (b + 1) * P)
                            mm = three_products(pe, aux[:, 2 * b + h, :],
                                                [(w_h[:, c, feats], w_l[:, c, feats],
                                                  attn_hi[:, c, cols], attn_lo[:, c, cols])
                                                 for c in range(HEADS)])
                        mm.then_inc(*((branch_a_half, 1) if b == 0 else (multiplied[PH_A.slots[k]], 1)))

            for k in range(6):
                p = k // 2
                pe.wait_ge(mix_lo_ready, 2 * p + 2)
                row_unit(pe, PH_WO, 0, k, mix_hi[:, 2 * p:2 * p + 2, :], mix_lo[:, 2 * p:2 * p + 2, :], k)
            pe.wait_ge(mix_lo_ready, KC)
            for j, (u, t) in enumerate(PAIR_ORDER):
                row_tile(pe, PH_WO, 0, 6 + u, mix_hi[:, 6:8, :], mix_lo[:, 6:8, :], t, j, 6)
                if u == 1 and t >= 2:
                    norm_turn(pe, 1, t - 2, xn2[:, (t - 2) % 4, :])

            pe.wait_ge(norm_sem[1]["lo"], 4)
            feature_half(pe, PH_F0, 0, 0, h2_hi, h2_lo, 0)
            norm_turn(pe, 1, 6, xn2[:, 2, :])
            norm_turn(pe, 1, 7, xn2[:, 3, :])
            feature_half(pe, PH_F0, 0, 1, h2_hi, h2_lo, 0)
            pe.wait_ge(norm_sem[1]["lo"], TT)
            feature_half(pe, PH_F0, 0, 0, h2_hi, h2_lo, 1)
            feature_half(pe, PH_F0, 0, 1, h2_hi, h2_lo, 1)
            for k in range(2, 4):
                feature_unit(pe, PH_F0, 0, k, h2_hi, h2_lo)
            with pe.Fori(0, FFN_LOOPS) as i:
                feature_unit(pe, PH_F, i, F_G0, h2_hi, h2_lo)
                pe.wait_ge(act_lo_ready, i * 2 + 2)
                row_unit(pe, PH_F, i, F_DA, act_hi[0], act_lo[0], i * 2 + ROWS_FFN)
                row_unit(pe, PH_F, i, F_DB, act_hi[0], act_lo[0], i * 2 + (ROWS_FFN + 1))
                feature_unit(pe, PH_F, i, F_U0, h2_hi, h2_lo)
                feature_unit(pe, PH_F, i, F_G1, h2_hi, h2_lo)
                feature_unit(pe, PH_F, i, F_U1, h2_hi, h2_lo)
            for k in range(4):
                feature_unit(pe, PH_F1, 0, k, h2_hi, h2_lo)
            for k in range(4, 6):
                row_unit(pe, PH_F1, 0, k, act_hi[0], act_lo[0], ROWS_LAST - 2 + (k - 4))
            pe.wait_ge(act_lo_ready, 2 * FFN_LOOPS + 4)
            for j, (u, t) in enumerate(PAIR_ORDER):
                row_tile(pe, PH_F1, 0, 6 + u, act_hi[1], act_lo[1], t, j, ROWS_LAST)

        @block.scalar
        def _(act):
            for b in range(2):
                act.sem_inc(out_read[b], 1)
            act.wait_ge(const_set, 2)
            def round_gate_weights(i):
                act.wait_ge(gate_weights_loaded, i * 32 + 32)
                act.activation(w_gate_parts[:, :], w_gate_head[:, :], ACT.Copy).then_inc(gate_weights_rounded, 1)

            def copy_v(i, b):
                act.activation(v_tok[:, 4 * b:4 * b + 4, :], proj[b][:, :].rearrange("p (t n) -> p t n", n=GV),
                               ACT.Copy).then_inc(v_read, 1)
                act.wait_ge(v_read, i * 2 + (b + 1))
                act.sem_inc(out_read[b], 1)

            act.activation(small[:, 2:3], eps, ACT.Sqrt, bias=eps)
            for t in range(TT + 1):
                if t < TT:
                    act.wait_ge(x_loaded[t], 16)
                    norm_root(act, 0, t, x_in[:, t, :], square1, ss1, rms1)
                if t >= 1:
                    norm_hi(act, 0, t - 1, ht_hi)
                if t == 1:
                    round_unit(act, PH_GLA, 0, G_V0)
                if t == 2:
                    round_unit(act, PH_GLA, 0, G_V1)
                if t == 6:
                    act.wait_ge(glr_loaded, 16)
                    act.activation(glr_weights[:, :, :, 0, :], glr_raw_four, ACT.Copy).then_inc(glr_rounded, 1)
                    round_gate_weights(0)
                if t == 7:
                    act.wait_ge(v_half_done, 1)
                    copy_v(0, 0)
            act.wait_ge(glr_done, 1)
            act.activation(glr_t[:, :], aux_a, ACT.Copy).then_inc(glr_hi_ready, 1)
            round_unit(act, PH_GLA, 0, G_K)
            round_unit(act, PH_GLA, 0, G_Q)
            copy_v(0, 1)

            def gla_head(i, first):
                def round_next(k):
                    if k + 2 < 6:
                        round_unit(act, PH_GLA, i, k + 2)
                    else:
                        round_unit(act, PH_GLA, i + 1, k - 4)

                def done(k):
                    unit_multiplied(act, PH_GLA, i, k)

                if not first:
                    round_gate_weights(i)
                    round_next(G_V0)
                act.wait_ge(z_done, i + 1)
                act.activation(diff1[:, :], aux_a, ACT.Abs, bias=b_gate_head).then_inc(soft_step, 1)
                act.wait_ge(soft_step, i * 2 + 1)
                act.activation(diff1[:, :], diff1[:, :], ACT.Exp, scale=-1.0).then_inc(soft_step, 1)
                act.wait_ge(soft_step, i * 2 + 2)
                act.activation(diff1[:, :], diff1[:, :], ACT.Ln, bias=one).then_inc(soft_ready, 1)
                if not first:
                    act.wait_ge(v_half_done, i + 1)
                    copy_v(i, 0)
                    round_next(G_V1)
                    done(G_V1)
                    copy_v(i, 1)
                act.wait_ge(diffs_ready, i + 1)
                act.activation(exp_a[:, :], diff1[:, :], ACT.Exp, scale=-1.0 / GATE_NORM)
                act.activation(exp_b[:, :], diff2[:, :], ACT.Exp, scale=1.0 / GATE_NORM)
                act.activation(decay, b_cum[:, CH - 1:S:CH], ACT.Exp, scale=1.0 / GATE_NORM)\
                   .then_inc(k_exps_ready, 1)
                round_next(G_K)
                act.wait_ge(k_scaled, i + 1)
                act.activation(exp_a[:, :], diff1[:, :], ACT.Exp, scale=1.0 / GATE_NORM)
                act.activation(exp_b[:, :], b_cum[:, :], ACT.Exp, scale=1.0 / GATE_NORM)\
                   .then_inc(q_exps_ready, 1)
                round_next(G_Q)
                act.wait_ge(gla_turned, i + 1)
                act.activation(k_tok[:, :, :], aux_b.rearrange("p (t n) -> p t n", t=TT), ACT.Copy)\
                   .then_inc(gla_turn_read, 1)
                round_next(G_R0)
                done(G_R0)
                act.activation(gla_silu[:, 0, :], proj[0][:, :], ACT.Silu).then_inc(gate_r_ready, 1)
                act.wait_ge(gate_r_ready, i * 2 + 1)
                act.sem_inc(out_read[0], 1)
                for t in range(TT):
                    act.wait_ge(o_done, i * TT + (t + 1))
                    if t:
                        act.wait_ge(gla_squared, i * TT + t)
                    act.activation(square_g[:, :], output_psum(t), ACT.Square,
                                   accum_out=ssg[:, t:t + 1]).then_inc(gla_squared, 1)
                    act.activation(o_tok[:, t, :], output_psum(t), ACT.Copy).then_inc(o_read, 1)
                act.wait_ge(gla_squared, i * TT + TT)
                act.activation(rmsg, ssg, ACT.Sqrt, bias=eps, scale=1.0 / GV).then_inc(gla_root, 1)
                round_next(G_R1)
                done(G_R1)
                act.activation(gla_silu[:, 1, :], proj[1][:, :], ACT.Silu).then_inc(gate_r_ready, 1)
                act.wait_ge(gate_r_ready, i * 2 + 2)
                act.sem_inc(out_read[1], 1)

            gla_head(0, True)
            with act.Fori(1, HEADS) as i:
                gla_head(i, False)

            act.wait_ge(gla_written, 2 * HEADS + 1)
            for c in range(KC):
                act.activation(gla_hi[:, c, :], gla_raw[:, c, :], ACT.Copy).then_inc(gla_hi_ready, 1)
            with act.Fori(0, KC) as i:
                round_unit(act, PH_B, i + 1, 0)
                unit_multiplied(act, PH_B, i, 0)
                act.wait_ge(out_read[1], PH_B.o(i, 1) + 1)
                act.activation(gate_b[:, :], proj[0][:, :], ACT.Sigmoid).then_inc(out_read[0], 1)
                round_unit(act, PH_B, i + 1, 1)

            with act.Fori(0, HEADS) as i:
                def round_next(k):
                    if k + 2 < 9:
                        round_unit(act, PH_ATT, i, k + 2)

                def exps(g):
                    act.wait_ge(neg_max_ready, i * 3 + (g + 1))
                    for t, (_, tile, off, width) in enumerate([x for x in score_tiles() if x[0] == g]):
                        part = prob[g][:, off:off + width]
                        act.activation(part, part, ACT.Exp, bias=neg_max[:, g, tile:tile + 1],
                                       scale=HD ** -0.5, accum_out=own_stats[:, g, tile, 1:2])\
                           .then_inc(exps_done, 1)

                def copy_values(g):
                    act.wait_ge(va_turned, i * 3 + (g + 1))
                    bank = (0, 2, 0)[g]
                    act.activation(va_tok[:, g, :, :], aux[:, bank:bank + 2, :].rearrange(
                        "p a (t n) -> p (a t) n", n=HD), ACT.Copy).then_inc(va_tok_ready, 1)

                for k in range(9):
                    round_next(k)
                    if k == 7:
                        exps(2)
                    if k == 8:
                        copy_values(1)
                    unit_multiplied(act, PH_ATT, i, k)
                    if k < 6:
                        act.activation(qkv[k % 3][:, :], proj[k % 2][:, :], ACT.Copy).then_inc(qk_copied, 1)
                        if k in (3, 5):
                            exps(k // 2 - 1)
                    else:
                        act.activation(qkv[k - 6][:, :], proj[k % 2][:, :], ACT.Copy).then_inc(va_ready, 1)
                        act.wait_ge(va_ready, i * 3 + (k - 5))
                        act.sem_inc(out_read[k % 2], 1)
                        if k == 7:
                            copy_values(0)
                            act.wait_ge(combine_step, i * 5 + 2)
                            act.activation(scaled[:, :, :], shifted[:, :, :], ACT.Exp, scale=HD ** -0.5)\
                               .then_inc(shift_exp_ready, 1)
                for c in range(9):
                    act.wait_ge(prob_turned, i * 9 + (c + 1))
                    n = min(4, len(prob_blocks()) - 4 * c) * P
                    act.activation(prob_t[:, c % 3, 0:n], aux[:, 2 + c % 2, 0:n], ACT.Copy)\
                       .then_inc(prob_t_ready, 1)
                    if c == 1:
                        copy_values(2)
                    if c in (2, 4):
                        round_unit(act, PH_ATT, i + 1, c // 2 - 1)
                act.wait_ge(pv_done, i + 1)
                act.activation(attn_raw[:, bass.ds(i, 1), :], proj[1][:, :].rearrange("p (a s) -> p a s", a=1),
                               ACT.Copy).then_inc(attn_written, 1)
                act.wait_ge(attn_written, i * 2 + 2)
                act.sem_inc(out_read[1], 1)

            act.wait_ge(attn_written, 2 * HEADS + 1)
            for c in range(HEADS):
                act.activation(attn_hi[:, c, :], attn_raw[:, c, :], ACT.Copy).then_inc(attn_hi_ready, 1)
            with act.Fori(0, 2) as i:
                def mix_hi_block(m, b):
                    act.wait_ge(gated_a, i * 4 + (2 * m + b + 3))
                    act.activation(mix_hi[:, bass.ds(i * 4 + (2 * m + b), 1), :],
                                   mix[:, bass.ds(i * 4 + (2 * m + b), 1), :], ACT.Copy)\
                       .then_inc(mix_hi_ready, 1)

                for k in range(6):
                    if k % 3 == 2:
                        mix_hi_block(k // 3, 0)
                    if k < 4:
                        round_unit(act, PH_A, i, k + 2)
                    else:
                        round_unit(act, PH_A, i + 1, k - 4)
                    if k % 3 == 2:
                        mix_hi_block(k // 3, 1)
                    if k % 3 < 2:
                        unit_multiplied(act, PH_A, i, k)
                        act.wait_ge(gated_a, i * 4 + (k // 3 * 2 + k % 3 + 1))
                        act.activation(gate_a[:, k % 3, :], proj[PH_A.outs[k]][:, :], ACT.Sigmoid)\
                           .then_inc(out_read[PH_A.outs[k]], 1)

            for k in range(6):
                round_unit(act, PH_WO, 0, k + 2)
            for t in range(TT + 2):
                if t == TT - 2:
                    round_unit(act, PH_F0, 0, 0)
                if t < TT:
                    pair_added(act, t, 6)
                    norm_root(act, 1, t, x2[:, t, :], square2, ss2, rms2)
                if t >= 2:
                    norm_hi(act, 1, t - 2, h2_hi)
                if t == TT - 1:
                    round_unit(act, PH_F0, 0, 1)

            def silu(ph, i, k, part_use):
                unit_multiplied(act, ph, i, k)
                act.wait_ge(gated_ready, part_use)
                act.activation(silu_g[:, :], proj[0][:, :], ACT.Silu).then_inc(out_read[0], 1)

            def act_hi_block(count, b, place=0):
                act.wait_ge(gated_ready, count + 1)
                act.activation(act_hi[place][:, b, :], gated[:, :], ACT.Copy).then_inc(act_hi_ready, 1)

            for k in range(4):
                if k < 2:
                    round_unit(act, PH_F0, 0, k + 2)
                else:
                    round_unit(act, PH_F, 0, k - 2)
                if k % 2 == 0:
                    silu(PH_F0, 0, k, k // 2 + 1)
                else:
                    act_hi_block(k // 2 + 1, k // 2)
            with act.Fori(0, FFN_LOOPS) as i:
                round_unit(act, PH_F, i, F_DB)
                silu(PH_F, i, F_G0, i * 2 + 3)
                round_unit(act, PH_F, i, F_U0)
                round_unit(act, PH_F, i, F_G1)
                round_unit(act, PH_F, i, F_U1)
                act_hi_block(i * 2 + 3, 0)
                round_unit(act, PH_F, i + 1, 0)
                silu(PH_F, i, F_G1, i * 2 + 4)
                round_unit(act, PH_F, i + 1, 1)
                act_hi_block(i * 2 + 4, 1)
            for k in range(4):
                round_unit(act, PH_F1, 0, k + 2)
                if k % 2 == 0:
                    silu(PH_F1, 0, k, 2 * FFN_LOOPS + 3 + k // 2)
                else:
                    act_hi_block(2 * FFN_LOOPS + 3 + k // 2, k // 2, 1)
            for k in range(6, 8):
                round_unit(act, PH_F1, 0, k)
            for t in range(TT):
                pair_added(act, t, ROWS_LAST)
                norm_root(act, 2, t, x2[:, t, :], square2, ss3, rms3)

        @block.vector
        def _(dve):
            for s in range(2):
                dve.sem_inc(split[s], 1)
            dve.sem_inc(rows_added, 4)
            dve.sem_inc(gla_written, 1)
            dve.sem_inc(prob_t_ready, 1)
            dve.sem_inc(attn_written, 1)
            dve.sem_inc(gated_ready, 1)
            dve.sem_inc(gate_a_step, 2)
            dve.sem_inc(gated_a, 2)
            def split_gate_weights(i):
                dve.wait_ge(gate_weights_rounded, i + 1)
                for row in (2 * RANK, 6 * RANK):
                    rows = slice(row, row + 2 * RANK)
                    dve.tensor_tensor(w_gate_parts[rows, :], w_gate_head[rows, :],
                                      w_gate_parts[rows, :].bitcast(F32), ALU.subtract)\
                       .then_inc(gate_weights_split, 1)

            dve.wait_ge(gain1_loaded, 16)
            for t in range(TT + 1):
                if t < TT:
                    if t >= 4:
                        dve.wait_ge(norm_sem[0]["turned"], t - 3)
                    norm_scale(dve, 0, t, x_in[:, t, :], rms1, rstd1, gain1, xn[:, t % 4, :])
                if t >= 1:
                    norm_lo(dve, 0, t - 1, ht_hi, ht_lo)
                if t == 1:
                    split_unit(dve, PH_GLA, 0, G_V0)
                if t == 2:
                    split_unit(dve, PH_GLA, 0, G_V1)
                if t == 7:
                    dve.wait_ge(glr_rounded, 1)
                    dve.tensor_tensor(glr_weights[:, :, :, 1, :], glr_raw_four,
                                      glr_weights[:, :, :, 0, :].bitcast(F32), ALU.subtract)\
                       .then_inc(glr_split, 1)
                    split_gate_weights(0)
            dve.wait_ge(glr_hi_ready, 1)
            low = slice(P // 2, P)
            dve.tensor_tensor(glr_t[low, :], aux_a[low, :], glr_t[low, :].bitcast(F32), ALU.subtract)\
               .then_inc(glr_ready, 1)
            split_unit(dve, PH_GLA, 0, G_K)
            split_unit(dve, PH_GLA, 0, G_Q)
            dve.wait_ge(masks_loaded, 16)
            dve.wait_ge(gla_gain_loaded, 16)
            dve.memset(att_t[:, :, :], 0.0).then_inc(att_t_cleared, 1)

            def gla_head(i, first):
                def split_next(k):
                    if k + 2 < 6:
                        split_unit(dve, PH_GLA, i, k + 2)
                    else:
                        split_unit(dve, PH_GLA, i + 1, k - 4)

                chunks = b_cum[:, :].rearrange("p (c j) -> p c j", j=CH)
                d1 = diff1[:, :].rearrange("p (c j) -> p c j", j=CH)
                d2 = diff2[:, :].rearrange("p (c j) -> p c j", j=CH)
                wide = [P, S // CH, CH]

                def by_chunk(ap):
                    return ap[:, :].rearrange("p (t c j) -> p t c j", c=2, j=CH)

                if not first:
                    split_gate_weights(i)
                    split_next(G_V0)
                dve.wait_ge(soft_step, i * 2 + 1)
                dve.tensor_scalar(diff2[:, :], aux_a, b_gate_head, 0.0, ALU.add, ALU.min)\
                   .then_inc(z_clamped, 1)
                dve.wait_ge(z_clamped, i + 1)
                dve.wait_ge(soft_ready, i + 1)
                dve.tensor_tensor(diff2[:, :], diff2[:, :], diff1[:, :], ALU.subtract).then_inc(log_a_ready, 1)
                dve.wait_ge(log_a_ready, i + 1)
                for h in range(2):
                    cols = slice(h * HALF, (h + 1) * HALF)
                    dve.tensor_tensor_scan(b_cum[:, cols], restart, diff2[:, cols], 0.0, ALU.mult, ALU.add)\
                       .then_inc(cumsum_done, 1)
                dve.wait_ge(cumsum_done, i * 2 + 2)
                dve.tensor_tensor(d1, chunks, chunks[:, :, CH // 2:CH // 2 + 1].to_broadcast(wide), ALU.subtract)
                dve.tensor_tensor(d2, chunks[:, :, CH - 1:CH].to_broadcast(wide), chunks, ALU.subtract)\
                   .then_inc(diffs_ready, 1)
                if not first:
                    split_next(G_V1)
                split_next(G_K)
                unit_multiplied(dve, PH_GLA, i, G_K)
                dve.wait_ge(k_exps_ready, i + 1)
                k_ps, k_last, e_b = by_chunk(proj[0]), by_chunk(k_end), by_chunk(exp_b)
                half = [P, TT, CH]
                dve.tensor_tensor(decay_two, decay[:, 0:16:2], decay[:, 1:16:2], ALU.mult)
                dve.tensor_tensor(k_cross[:, :, :], k_ps[:, :, 0, :], e_b[:, :, 0, :], ALU.mult)\
                   .then_inc(cross_ready, 1)
                dve.tensor_tensor(k_last[:, :, 1, :], k_ps[:, :, 1, :], e_b[:, :, 1, :], ALU.mult)
                dve.tensor_tensor(k_dec[:, :], proj[0][:, :], exp_a[:, :], ALU.mult).then_inc(k_read, 1)
                dve.wait_ge(k_read, i + 1)
                dve.sem_inc(out_read[0], 1)
                dve.wait_ge(cross_ready, i + 1)
                dve.tensor_tensor(k_last[:, :, 0, :], k_cross[:, :, :],
                                  decay[:, 1:16:2].rearrange("p (t a) -> p t a", a=1).to_broadcast(half),
                                  ALU.mult).then_inc(k_scaled, 1)
                split_next(G_Q)
                unit_multiplied(dve, PH_GLA, i, G_Q)
                dve.wait_ge(q_exps_ready, i + 1)
                q_ps, q_start = by_chunk(proj[1]), by_chunk(q_int)
                for dst, src, e in ((q_cross[:, :, :], q_ps[:, :, 1, :], e_b[:, :, 1, :]),
                                    (q_start[:, :, 0, :], q_ps[:, :, 0, :], e_b[:, :, 0, :]),
                                    (q_dec[:, :], proj[1][:, :], exp_a[:, :])):
                    dve.scalar_tensor_tensor(dst, src, float(P) ** -0.5, e, ALU.mult, ALU.mult)\
                       .then_inc(q_read, 1)
                dve.wait_ge(q_read, i * 3 + 3)
                dve.sem_inc(out_read[1], 1)
                dve.tensor_tensor(q_start[:, :, 1, :], q_cross[:, :, :],
                                  decay[:, 0:16:2].rearrange("p (t a) -> p t a", a=1).to_broadcast(half),
                                  ALU.mult).then_inc(q_scaled, 1)
                split_next(G_R0)
                wait_apart(dve, att_t_done, i + 1)
                def mask_bank(h):
                    dve.copy_predicated(att_t[:, 4 * h:4 * h + 4, :],
                                        gla_mask.bitcast(I32).rearrange("p (a n) -> p a n", a=1)
                                        .to_broadcast([P, 4, P]),
                                        aux[:, h, :].rearrange("p (t n) -> p t n", t=4)).then_inc(att_t_ready, 1)
                mask_bank(0)
                for t in range(TT - 1):
                    if t == 1:
                        mask_bank(1)
                    dve.wait_ge(update_done, i * 7 + (t + 1))
                    if t >= 3:
                        dve.wait_ge(o_done, i * TT + (t - 2))
                    new, upd = state[:, (t + 1) % 4, :], aux[:, 2 + t % 2, 0:GV]
                    if t == 0:
                        dve.tensor_copy(new, upd).then_inc(state_ready, 1)
                    else:
                        dve.wait_ge(state_ready, i * 7 + t)
                        dve.scalar_tensor_tensor(new, state[:, t % 4, :], decay_two[:, t:t + 1], upd,
                                                 ALU.mult, ALU.add).then_inc(state_ready, 1)
                dve.wait_ge(gla_root, i + 1)
                dve.reciprocal(rstdg, rmsg).then_inc(gla_recip, 1)
                dve.wait_ge(gla_recip, i + 1)
                dve.tensor_tensor(o_tok[:, :, :], o_tok[:, :, :],
                                  rstdg.rearrange("p (t a) -> p t a", a=1).to_broadcast([P, TT, GV]),
                                  ALU.mult).then_inc(o_normed, 1)
                split_next(G_R1)
                for v, src in enumerate((aux_a, aux_b)):
                    dve.wait_ge(o_turned, i * 2 + (v + 1))
                    dve.wait_ge(gate_r_ready, i * 2 + (v + 1))
                    dve.scalar_tensor_tensor(gla_raw[:, bass.ds(i * 2 + v, 1), :],
                                             src.rearrange("p (a s) -> p a s", a=1), gla_gain[:, v:v + 1],
                                             gla_silu[:, v:v + 1, :], ALU.mult, ALU.mult)\
                       .then_inc(gla_written, 1)

            gla_head(0, True)
            with dve.Fori(1, HEADS) as i:
                gla_head(i, False)

            for c in range(KC):
                dve.wait_ge(gla_hi_ready, c + 1)
                dve.tensor_tensor(gla_lo[:, c, :], gla_raw[:, c, :], gla_hi[:, c, :].bitcast(F32),
                                  ALU.subtract).then_inc(gla_lo_ready, 1)
            with dve.Fori(0, KC) as i:
                split_unit(dve, PH_B, i + 1, 0)
                split_unit(dve, PH_B, i + 1, 1)
                dve.wait_ge(out_read[0], PH_B.o(i, 0) + 2)
                dve.tensor_tensor(mix[:, bass.ds(i, 1), :], proj[1][:, :].rearrange("p (a s) -> p a s", a=1),
                                  gate_b[:, :].rearrange("p (a s) -> p a s", a=1), ALU.mult)\
                   .then_inc(out_read[1], 1)

            dve.wait_ge(out_read[1], PH_B.out_end[1] + 1)
            dve.wait_ge(rope_loaded, 16)
            swap = list(range(16, 32)) + list(range(16))
            with dve.Fori(0, HEADS) as i:
                def split_next(k):
                    if k + 2 < 9:
                        split_unit(dve, PH_ATT, i, k + 2)
                    elif k == 8:
                        split_unit(dve, PH_ATT, i + 1, 0)
                        split_unit(dve, PH_ATT, i + 1, 1)

                def rotate(k):
                    src, dst = proj[k % 2][0:ROPE, :], qkv[k % 3][0:ROPE, :]
                    wait_apart(dve, qk_copied, i * 6 + (k + 1))
                    if k:
                        wait_apart(dve, qk_ready, i * 6 + k)
                    dve.stream_shuffle(rotated[:, :], src, swap).then_inc(rope_step, 1)
                    dve.wait_ge(rope_step, i * 18 + (3 * k + 1))
                    dve.tensor_tensor(rotated[:, :], rotated[:, :], rope_sb[:, 1, :], ALU.mult)\
                       .then_inc(rope_step, 1)
                    dve.tensor_tensor(dst, src, rope_sb[:, 0, :], ALU.mult).then_inc(rope_step, 1)
                    dve.wait_ge(rope_step, i * 18 + (3 * k + 3))
                    dve.sem_inc(out_read[k % 2], 1)
                    dve.tensor_tensor(dst, dst, rotated[:, :], ALU.add).then_inc(qk_ready, 1)

                def mask_scores(g):
                    for n, (_, t, off, width) in enumerate([x for x in score_tiles() if x[0] == g]):
                        wait_apart(dve, scores_done, i * 24 + (8 * g + n // 2 * 2 + 2))
                        mask = pair if g == 2 else band[:, 2 * P - width:2 * P]
                        dve.tensor_tensor_reduce(prob[g][:, off:off + width],
                                                 aux[:, n // 2, n % 2 * 2 * P:n % 2 * 2 * P + width], mask,
                                                 1.0, -3.0e38, ALU.add, ALU.max,
                                                 own_stats[:, g, t, 0:1]).then_inc(scores_masked, 1)
                    dve.wait_ge(scores_masked, i * 24 + (8 * g + 8))
                    dve.tensor_scalar(neg_max[:, g, :], own_stats[:, g, :, 0], -(HD ** -0.5), None, ALU.mult)\
                       .then_inc(neg_max_ready, 1)

                for k in range(9):
                    split_next(k)
                    if k < 6:
                        rotate(k)
                    if k in (2, 4, 6):
                        mask_scores(k // 2 - 1)
                    if k == 7:
                        for g in range(GROUPS):
                            dve.wait_ge(stats_back[g], i * (16, 64, 16)[g] + (16, 64, 16)[g])
                        every = all_stats[:, :, :, :].rearrange("p y t (g s) -> p (y t) g s", s=2)
                        dve.tensor_reduce(top[:, :], every[:, :, :, 0], AX.X, ALU.max).then_inc(combine_step, 1)
                        dve.wait_ge(combine_step, i * 5 + 1)
                        dve.tensor_tensor(shifted[:, :, :], every[:, :, :, 0],
                                          top[:, :].rearrange("p (y a) -> p y a", a=1)
                                          .to_broadcast([P, GROUPS * TT, GROUPS]), ALU.subtract)\
                           .then_inc(combine_step, 1)
                        dve.wait_ge(shift_exp_ready, i + 1)
                        dve.tensor_tensor(shifted[:, :, :], scaled[:, :, :], every[:, :, :, 1], ALU.mult)\
                           .then_inc(combine_step, 1)
                        dve.wait_ge(combine_step, i * 5 + 3)
                        dve.tensor_reduce(total[:, :], shifted[:, :, :], AX.X, ALU.add).then_inc(combine_step, 1)
                        dve.wait_ge(combine_step, i * 5 + 4)
                        dve.reciprocal(top[:, :], total[:, :]).then_inc(combine_step, 1)
                        dve.wait_ge(combine_step, i * 5 + 5)
                        own = scaled[:, :, :].rearrange("p (y t) g -> p y t g", y=GROUPS)
                        for g in range(GROUPS):
                            dve.tensor_tensor(weight[:, g, :], own[:, g, :, g], top[:, g * TT:(g + 1) * TT],
                                              ALU.mult).then_inc(weight_ready, 1)
                        for n, (g, t, off, width) in enumerate(score_tiles()):
                            if t == 0 and g < 3 and n % 8 == 0:
                                dve.wait_ge(weight_ready, i * 3 + (g + 1))
                            part = prob[g][:, off:off + width]
                            dve.tensor_scalar(part, part, weight[:, g, t:t + 1], None, ALU.mult)\
                               .then_inc(prob_weighted, 1)
                dve.wait_ge(attn_written, i * 2 + 2)
                head = attn_raw[:, bass.ds(i, 1), :].rearrange("p a (q t) -> p (a t) q", t=TT)
                dve.tensor_tensor(head, head, aux_a.rearrange("p (t q) -> p t q", t=TT), ALU.add)\
                   .then_inc(attn_written, 1)

            for c in range(HEADS):
                dve.wait_ge(attn_hi_ready, c + 1)
                dve.tensor_tensor(attn_lo[:, c, :], attn_raw[:, c, :], attn_hi[:, c, :].bitcast(F32),
                                  ALU.subtract).then_inc(attn_lo_ready, 1)
            with dve.Fori(0, 2) as i:
                def gate_block(m, b):
                    k = 3 * m + b
                    dve.wait_ge(out_read[PH_A.outs[k]], PH_A.o(i, k) + 2)
                    gate = gate_a[:, b:b + 1, :]
                    dve.tensor_tensor(gate, aux[:, 2 * b:2 * b + 2, :].rearrange("p (a h) s -> p a (h s)", a=1),
                                      gate, ALU.mult).then_inc(gate_a_step, 1)
                    dve.wait_ge(gate_a_step, i * 4 + (2 * m + b + 3))
                    dst = mix[:, bass.ds(i * 4 + (2 * m + b), 1), :]
                    dve.tensor_tensor(dst, dst, gate, ALU.add).then_inc(gated_a, 1)

                def mix_lo_block(m, b):
                    block_at = bass.ds(i * 4 + (2 * m + b), 1)
                    dve.wait_ge(mix_hi_ready, i * 4 + (2 * m + b + 1))
                    dve.tensor_tensor(mix_lo[:, block_at, :], mix[:, block_at, :],
                                      mix_hi[:, block_at, :].bitcast(F32), ALU.subtract)\
                       .then_inc(mix_lo_ready, 1)

                for k in range(6):
                    m = k // 3
                    if k % 3 == 2:
                        dve.wait_ge(branch_a_half, i * 2 + (m + 1))
                        gate_block(m, 0)
                        mix_lo_block(m, 0)
                        unit_multiplied(dve, PH_A, i, k)
                        gate_block(m, 1)
                    if k < 4:
                        split_unit(dve, PH_A, i, k + 2)
                    else:
                        split_unit(dve, PH_A, i + 1, k - 4)
                    if k % 3 == 2:
                        mix_lo_block(m, 1)

            for k in range(6):
                add_rows(dve, PH_WO, 0, k, k % 2, k)
                split_unit(dve, PH_WO, 0, k + 2)
            dve.wait_ge(gains_loaded, 16)

            def scale2(t):
                if t >= 4:
                    dve.wait_ge(norm_sem[1]["turned"], t - 3)
                norm_scale(dve, 1, t, x2[:, t, :], rms2, rstd2, gain2, xn2[:, t % 4, :])

            for j, (u, t) in enumerate(PAIR_ORDER):
                add_pair_tile(dve, PH_WO, 6, j, 6)
                if (u, t) == (1, TT - 2):
                    split_unit(dve, PH_F0, 0, 0)
                if u == 1 and t >= 1:
                    scale2(t - 1)
                if u == 1 and t >= 3:
                    norm_lo(dve, 1, t - 3, h2_hi, h2_lo)
            scale2(TT - 1)
            for t in range(TT - 3, TT):
                norm_lo(dve, 1, t, h2_hi, h2_lo)
                if t == TT - 3:
                    split_unit(dve, PH_F0, 0, 1)

            def hidden(ph, i, k, count, b, place=0):
                if not isinstance(count, int) or count > 1:
                    dve.wait_ge(act_lo_ready, count - 1)
                unit_multiplied(dve, ph, i, k)
                dve.wait_ge(out_read[0], ph.o(i, k - (3 if ph is PH_F and k == F_U0 else 1)) + 2)
                dve.tensor_tensor(gated[:, :], proj[1][:, :], silu_g[:, :], ALU.mult).then_inc(gated_ready, 1)
                dve.wait_ge(gated_ready, count + 1)
                dve.sem_inc(out_read[1], 1)
                if place == 0 or b == 0:
                    hidden_lo(count, b, place)

            def hidden_lo(count, b, place):
                dve.wait_ge(act_hi_ready, count)
                dve.tensor_tensor(act_lo[place][:, b, :], gated[:, :], act_hi[place][:, b, :].bitcast(F32), ALU.subtract)\
                   .then_inc(act_lo_ready, 1)

            for k in range(4):
                if k < 2:
                    split_unit(dve, PH_F0, 0, k + 2)
                else:
                    split_unit(dve, PH_F, 0, k - 2)
                if k % 2:
                    hidden(PH_F0, 0, k, k // 2 + 1, k // 2)
            with dve.Fori(0, FFN_LOOPS) as i:
                split_unit(dve, PH_F, i, F_DB)
                add_rows(dve, PH_F, i, F_DA, 0, i * 2 + ROWS_FFN)
                split_unit(dve, PH_F, i, F_U0)
                add_rows(dve, PH_F, i, F_DB, 1, i * 2 + (ROWS_FFN + 1))
                split_unit(dve, PH_F, i, F_G1)
                split_unit(dve, PH_F, i, F_U1)
                hidden(PH_F, i, F_U0, i * 2 + 3, 0)
                split_unit(dve, PH_F, i + 1, 0)
                split_unit(dve, PH_F, i + 1, 1)
                hidden(PH_F, i, F_U1, i * 2 + 4, 1)
            dve.wait_ge(gain_f_loaded, 16)
            for k in range(4):
                split_unit(dve, PH_F1, 0, k + 2)
                if k % 2:
                    hidden(PH_F1, 0, k, 2 * FFN_LOOPS + 3 + k // 2, k // 2, 1)
            for k in range(4, 6):
                add_rows(dve, PH_F1, 0, k, k - 4, ROWS_LAST - 2 + (k - 4))
                split_unit(dve, PH_F1, 0, k + 2)
                if k == 4:
                    hidden_lo(2 * FFN_LOOPS + 4, 1, 1)

            def scale_out(t):
                if t >= 4:
                    dve.wait_ge(out_stored[t % 4], 16)
                norm_scale(dve, 2, t, x2[:, t, :], rms3, rstd3, gain_f, out_sb[:, t % 4, :])

            for j, (u, t) in enumerate(PAIR_ORDER):
                add_pair_tile(dve, PH_F1, 6, j, ROWS_LAST)
                if u == 1 and 1 <= t < TT - 1:
                    scale_out(t - 1)
            scale_out(TT - 2)
            scale_out(TT - 1)


_INS = ["x", "norm1_g", "w_in", "w_gate_lr", "b_gate", "gla_norm_g", "w_branch_a", "w_branch_b",
        "w_out", "norm2_g", "w_ffn_in", "w_ffn_down", "norm_f_g"]
_OUTS = [((1, S, D), "float32")]


def kernel(**inputs):
    import concourse.bacc as _bacc
    from concourse.bass_utils import run_bass_kernel_spmd as _run

    nc = _bacc.Bacc("TRN2", target_bir_lowering=False, num_devices=1)
    arrays = {f"in_{name}_dram": np.ascontiguousarray(inputs[name]) for name in _INS}
    arrays["const_masks"], arrays["const_rope"] = shape_constants()
    args = [nc.dram_tensor(name, a.shape, mybir.dt.from_np(a.dtype), kind="ExternalInput").ap()
            for name, a in arrays.items()]
    for n, (shape, dtype) in enumerate(_OUTS):
        args.append(nc.dram_tensor(f"out_{n}_dram", shape, mybir.dt.from_np(np.dtype(dtype)),
                                   kind="ExternalOutput").ap())
    hybrid_block(nc, *args)
    r = _run(nc, [arrays], core_ids=[0])
    return r.results[0]["out_0_dram"]
```
